# Optimizing a Trainium2 kernel written in Bass

```python
import math
import jax
import jax.numpy as jnp
from jax import lax
import numpy as np

D_MODEL = 1024
BATCH = 1
SEQ = 1024
DEPTH = 2

CTX_LEN = 256
GRID_W = 64
N_MIXERS = 2
NA_HEADS = 16
NA_HEAD_DIM = D_MODEL // NA_HEADS
NA_WIN_ROWS = 8
NA_WIN_COLS = 16
DIFF_HEADS = 8
DIFF_HEAD_DIM = D_MODEL // (2 * DIFF_HEADS)
ROPE_THETA = 10000.0
Q_BLOCK = 128
N_EXPERTS = 16
N_GROUPS = 4
EXPERTS_PER_GROUP = N_EXPERTS // N_GROUPS
TOP_K = 2
D_EXPERT = 1024
N_MOD = 6
NORM_EPS = 1e-6
N_NA_LAYERS = (DEPTH + 1) // 2
N_DIFF_LAYERS = DEPTH // 2

kernel_name = "hybrid_natten_diffattn_grouped_moe_dit"

def rms_norm(x, g):
    xf = x.astype(jnp.float32)
    y = xf * lax.rsqrt(jnp.mean(xf * xf, axis=-1, keepdims=True) + NORM_EPS)
    return (y * g.astype(jnp.float32)).astype(x.dtype)

def modulate(h, shift, scale):
    return h * (1 + scale) + shift

def to_heads(t, n_heads, head_dim):
    b, n, _ = t.shape
    return t.reshape(b, n, n_heads, head_dim).transpose(0, 2, 1, 3)

def from_heads(t):
    b, h, n, d = t.shape
    return t.transpose(0, 2, 1, 3).reshape(b, n, h * d)

def axial_rope(n_tokens, head_dim):
    t = jnp.arange(n_tokens)
    row = (t // GRID_W).astype(jnp.float32)
    col = (t % GRID_W).astype(jnp.float32)
    n_freq = head_dim // 4
    inv_freq = ROPE_THETA ** (-jnp.arange(n_freq, dtype=jnp.float32) / n_freq)
    ang = jnp.concatenate([row[:, None] * inv_freq, col[:, None] * inv_freq], axis=-1)
    return jnp.cos(ang), jnp.sin(ang)

def apply_rope(x, cos, sin):
    cos = cos.astype(x.dtype)
    sin = sin.astype(x.dtype)
    x1, x2 = jnp.split(x, 2, axis=-1)
    return jnp.concatenate([x1 * cos - x2 * sin, x1 * sin + x2 * cos], axis=-1)

def dense_attention(q, k, v, scale):
    s = jnp.einsum("bhqd,bhkd->bhqk", q, k).astype(jnp.float32) * scale
    p = jax.nn.softmax(s, axis=-1).astype(v.dtype)
    return jnp.einsum("bhqk,bhkd->bhqd", p, v)

def neighbourhood_attention(hl, hc, w_qkv, w_o, rpb, ctx_out):
    b, s, _ = hl.shape
    rows = s // GRID_W
    wr = min(NA_WIN_ROWS, rows)
    n_band = wr * GRID_W
    scale = NA_HEAD_DIM ** -0.5
    ql, kl, vl = [to_heads(t, NA_HEADS, NA_HEAD_DIM) for t in jnp.split(hl @ w_qkv, 3, axis=-1)]
    qc, kc, vc = [to_heads(t, NA_HEADS, NA_HEAD_DIM) for t in jnp.split(hc @ w_qkv, 3, axis=-1)]
    kl_rows = kl.reshape(b, NA_HEADS, rows, GRID_W, NA_HEAD_DIM)
    vl_rows = vl.reshape(b, NA_HEADS, rows, GRID_W, NA_HEAD_DIM)
    q_blocks = ql.reshape(b, NA_HEADS, rows, GRID_W, NA_HEAD_DIM).transpose(2, 0, 1, 3, 4)
    row_ids = jnp.arange(rows)
    row_start = jnp.clip(row_ids - wr // 2, 0, rows - wr)
    col = jnp.arange(GRID_W)
    col_start = jnp.clip(col - NA_WIN_COLS // 2, 0, GRID_W - NA_WIN_COLS)
    in_window = (col[None, :] >= col_start[:, None]) & (col[None, :] < col_start[:, None] + NA_WIN_COLS)
    band_mask = jnp.broadcast_to(in_window[:, None, :], (GRID_W, wr, GRID_W)).reshape(GRID_W, n_band)
    n_dc = 2 * NA_WIN_COLS - 1
    dc_idx = jnp.clip(col[None, :] - col[:, None] + NA_WIN_COLS - 1, 0, n_dc - 1)
    rpb_flat = rpb.reshape(NA_HEADS, -1)

    def row_block(args):
        q, r, r0 = args
        k = lax.dynamic_slice_in_dim(kl_rows, r0, wr, axis=2).reshape(b, NA_HEADS, n_band, NA_HEAD_DIM)
        v = lax.dynamic_slice_in_dim(vl_rows, r0, wr, axis=2).reshape(b, NA_HEADS, n_band, NA_HEAD_DIM)
        dr_idx = r0 + jnp.arange(wr) - r + NA_WIN_ROWS - 1
        bias_idx = (dr_idx[None, :, None] * n_dc + dc_idx[:, None, :]).reshape(GRID_W, n_band)
        bias = rpb_flat[:, bias_idx].astype(jnp.float32)
        s_nb = jnp.einsum("bhqd,bhkd->bhqk", q, k).astype(jnp.float32) * scale + bias
        s_nb = jnp.where(band_mask, s_nb, -jnp.inf)
        s_ctx = jnp.einsum("bhqd,bhkd->bhqk", q, kc).astype(jnp.float32) * scale
        p = jax.nn.softmax(jnp.concatenate([s_nb, s_ctx], axis=-1), axis=-1).astype(v.dtype)
        return (jnp.einsum("bhqk,bhkd->bhqd", p[..., :n_band], v)
                + jnp.einsum("bhqk,bhkd->bhqd", p[..., n_band:], vc))

    o = lax.map(row_block, (q_blocks, row_ids, row_start))
    o = o.transpose(1, 2, 0, 3, 4).reshape(b, NA_HEADS, s, NA_HEAD_DIM)
    yl = from_heads(o) @ w_o
    yc = from_heads(dense_attention(qc, kc, vc, scale)) @ w_o if ctx_out else None
    return yl, yc

def diff_lambda_init(layer_idx):
    return 0.8 - 0.6 * math.exp(-0.3 * (layer_idx - 1))

def diff_attention(hl, hc, w_qkv, w_o, lam, subln_g, lam_init, cos, sin, ctx_out):
    b, s, _ = hl.shape
    scale = DIFF_HEAD_DIM ** -0.5

    def project(h):
        n = h.shape[1]
        q, k, v = jnp.split(h @ w_qkv, 3, axis=-1)
        q = q.reshape(b, n, DIFF_HEADS, 2, DIFF_HEAD_DIM).transpose(0, 2, 3, 1, 4)
        k = k.reshape(b, n, DIFF_HEADS, 2, DIFF_HEAD_DIM).transpose(0, 2, 3, 1, 4)
        v = to_heads(v, DIFF_HEADS, 2 * DIFF_HEAD_DIM)
        return q, k, v

    ql, kl, vl = project(hl)
    qc, kc, vc = project(hc)
    ql = apply_rope(ql, cos, sin)
    kl = apply_rope(kl, cos, sin)
    lam_f = lam.astype(jnp.float32)
    lam_full = jnp.exp(jnp.sum(lam_f[0] * lam_f[1])) - jnp.exp(jnp.sum(lam_f[2] * lam_f[3])) + lam_init

    def diff_map(q, k, v):
        sc = jnp.einsum("bhiqd,bhikd->bhiqk", q, k).astype(jnp.float32) * scale
        p = jax.nn.softmax(sc, axis=-1)
        a = (p[:, :, 0] - lam_full * p[:, :, 1]).astype(v.dtype)
        return jnp.einsum("bhqk,bhkd->bhqd", a, v)

    k_all = jnp.concatenate([kl, kc], axis=3)
    v_all = jnp.concatenate([vl, vc], axis=2)
    nb = s // Q_BLOCK
    q_blocks = ql.reshape(b, DIFF_HEADS, 2, nb, Q_BLOCK, DIFF_HEAD_DIM).transpose(3, 0, 1, 2, 4, 5)
    o = lax.map(lambda q: diff_map(q, k_all, v_all), q_blocks)
    o = o.transpose(1, 2, 0, 3, 4).reshape(b, DIFF_HEADS, s, 2 * DIFF_HEAD_DIM)

    def finish(t):
        return from_heads(rms_norm(t, subln_g) * (1 - lam_init)) @ w_o

    yl = finish(o)
    yc = finish(diff_map(qc, kc, vc)) if ctx_out else None
    return yl, yc

def grouped_moe(h, router_w, router_b, w_gate, w_up, w_down):
    t = h.shape[0]
    scores = jax.nn.sigmoid((h @ router_w).astype(jnp.float32))
    sel = (scores + router_b.astype(jnp.float32)).reshape(t, N_GROUPS, EXPERTS_PER_GROUP)
    group_score = jnp.sum(lax.top_k(sel, 2)[0], axis=-1)
    group = jnp.argmax(group_score, axis=-1)
    sel_in = jnp.take_along_axis(sel, group[:, None, None], axis=1)[:, 0]
    _, local = lax.top_k(sel_in, TOP_K)
    expert = group[:, None] * EXPERTS_PER_GROUP + local
    gate = jnp.take_along_axis(scores, expert, axis=-1)
    gate = gate / jnp.sum(gate, axis=-1, keepdims=True)
    flat_e = expert.reshape(-1)
    order = jnp.argsort(flat_e)
    tok = order // TOP_K
    sizes = jnp.bincount(flat_e, length=N_EXPERTS).astype(jnp.int32)
    xs = h[tok]
    a = lax.ragged_dot(xs, w_gate, sizes)
    u = lax.ragged_dot(xs, w_up, sizes)
    y = lax.ragged_dot(jax.nn.silu(a) * u, w_down, sizes)
    y = y * gate.reshape(-1)[order][:, None].astype(y.dtype)
    return jnp.zeros_like(h).at[tok].add(y.astype(h.dtype))

def setup_inputs(seed: int = 0) -> dict:
    key = jax.random.key(seed)
    ks = jax.random.split(key, 19)
    d = D_MODEL
    inv = d ** -0.5

    def normal(k, shape, std):
        return jax.random.normal(k, shape, jnp.float32) * std

    return {
        "x": normal(ks[0], (BATCH, SEQ, d), 1.0),
        "c": normal(ks[1], (BATCH, d), 1.0),
        "ctx": normal(ks[2], (BATCH, CTX_LEN, d), 1.0),
        "c_ctx": normal(ks[3], (d,), 1.0),
        "mod_w": normal(ks[4], (DEPTH, d, N_MOD * d), 0.5 * inv),
        "mod_b": normal(ks[5], (DEPTH, N_MOD * d), 0.02),
        "norm_mix": 1.0 + normal(ks[6], (DEPTH, d), 0.02),
        "norm_ffn": 1.0 + normal(ks[7], (DEPTH, d), 0.02),
        "w_qkv": normal(ks[8], (DEPTH, d, 3 * d), inv),
        "w_o": normal(ks[9], (DEPTH, d, d), inv),
        "na_rpb": normal(ks[10], (N_NA_LAYERS, NA_HEADS, 2 * NA_WIN_ROWS - 1, 2 * NA_WIN_COLS - 1), 0.1),
        "diff_lambda": normal(ks[11], (N_DIFF_LAYERS, 4, DIFF_HEAD_DIM), 0.1),
        "diff_subln": 1.0 + normal(ks[12], (N_DIFF_LAYERS, 2 * DIFF_HEAD_DIM), 0.02),
        "router_w": normal(ks[13], (d, N_EXPERTS), inv),
        "router_b": normal(ks[14], (N_EXPERTS,), 0.01),
        "expert_w_gate": normal(ks[15], (DEPTH, N_EXPERTS, d, D_EXPERT), inv),
        "expert_w_up": normal(ks[16], (DEPTH, N_EXPERTS, d, D_EXPERT), inv),
        "expert_w_down": normal(ks[17], (DEPTH, N_EXPERTS, D_EXPERT, d), D_EXPERT ** -0.5),
        "final_norm": 1.0 + normal(ks[18], (d,), 0.02),
    }

def reference(x, c, ctx, c_ctx, mod_w, mod_b, norm_mix, norm_ffn, w_qkv, w_o, na_rpb, diff_lambda,
              diff_subln, router_w, router_b, expert_w_gate, expert_w_up, expert_w_down, final_norm):
    b, s, d_model = x.shape
    cos, sin = axial_rope(s, DIFF_HEAD_DIM)
    c_act = jax.nn.silu(c)
    c_ctx_act = jax.nn.silu(c_ctx)
    xl, xc = x, ctx
    for i in range(DEPTH):
        last = i == DEPTH - 1
        mod_l = jnp.split((c_act @ mod_w[i] + mod_b[i])[:, None, :], N_MOD, axis=-1)
        mod_c = jnp.split((c_ctx_act @ mod_w[i] + mod_b[i])[None, None, :], N_MOD, axis=-1)
        hl = modulate(rms_norm(xl, norm_mix[i]), mod_l[0], mod_l[1])
        hc = modulate(rms_norm(xc, norm_mix[i]), mod_c[0], mod_c[1])
        j = i // N_MIXERS
        if i % N_MIXERS == 0:
            yl, yc = neighbourhood_attention(hl, hc, w_qkv[i], w_o[i], na_rpb[j], not last)
        else:
            yl, yc = diff_attention(hl, hc, w_qkv[i], w_o[i], diff_lambda[j], diff_subln[j],
                                    diff_lambda_init(i + 1), cos, sin, not last)
        xl = xl + mod_l[2] * yl
        hl = modulate(rms_norm(xl, norm_ffn[i]), mod_l[3], mod_l[4])
        if last:
            y = grouped_moe(hl.reshape(-1, d_model), router_w, router_b,
                            expert_w_gate[i], expert_w_up[i], expert_w_down[i])
            xl = xl + mod_l[5] * y.reshape(b, s, d_model)
        else:
            xc = xc + mod_c[2] * yc
            hc = modulate(rms_norm(xc, norm_ffn[i]), mod_c[3], mod_c[4])
            n_lat = b * s
            tokens = jnp.concatenate([hl.reshape(-1, d_model), hc.reshape(-1, d_model)], axis=0)
            y = grouped_moe(tokens, router_w, router_b, expert_w_gate[i], expert_w_up[i], expert_w_down[i])
            xl = xl + mod_l[5] * y[:n_lat].reshape(b, s, d_model)
            xc = xc + mod_c[5] * y[n_lat:].reshape(xc.shape)
    return rms_norm(xl, final_norm)


_drawn_inputs = setup_inputs


def setup_inputs(seed=0):
    import zlib

    import numpy as np

    out = dict(_drawn_inputs(seed))
    spreads = {}
    factors = {'norm_mix': 3.398, 'na_rpb': 4.908, 'diff_subln': 8.0, 'final_norm': 2.908}
    for name, (base, spread) in spreads.items():
        noise = np.random.default_rng([zlib.crc32(name.encode()), seed]).standard_normal(out[name].shape)
        drawn = base * np.exp(spread * noise) if base else spread * noise
        out[name] = jnp.asarray(drawn.astype(out[name].dtype))
    for name, factor in factors.items():
        out[name] = (out[name] * factor).astype(out[name].dtype)
    return out
```

```python
import math
from contextlib import ExitStack

import concourse.bass as bass
import numpy as np
from concourse import mybir

F32 = mybir.dt.float32
I32 = mybir.dt.int32
ACT = mybir.ActivationFunctionType
ALU = mybir.AluOpType
AX = mybir.AxisListType

P = 128
D = 1024
KD = D // P
SEQ, CTX = 1024, 256
LT, CT = SEQ // P, CTX // P
NT = LT + CT
NTOK = SEQ + CTX
GRID_W = 64
HALF = 512
NMOD = 6
NE, NG, EPG = 16, 4, 4
EPS = 1e-6
NEG = -1.0e30
HD = 64
SCALE = HD ** -0.5
GROUPS = D // P
WIN_ROWS, WIN_COLS = 8, 16
TABR = 14
INTR = 10
CAP = (160, 144)
TILES = (NT, LT)
ITEMS = tuple(NE + (2 * TILES[l] * P) // CAP[l] for l in range(2))
LAM_INIT = 0.8 - 0.6 * math.exp(-0.3 * (2 - 1))

C_ID, C_TRI, C_ONE, C_PERM = 0, 128, 256, 384
C_EDGE = 512
C_INT = C_EDGE + GRID_W
C_P4 = C_INT + INTR * GRID_W
C_P16 = C_P4 + NG
C_THR = C_P16 + NE
C_IOTA = C_THR + 16
C_HALF = C_IOTA + 64
C_ALL = C_HALF + 16


def shape_constants():
    c = np.zeros((P, C_ALL), np.float32)
    p = np.arange(P)
    c[:, C_ID:C_ID + P] = np.eye(P)
    c[:, C_TRI:C_TRI + P] = p[:, None] < p[None, :]
    c[:, C_ONE:C_ONE + P] = 1
    c[:, C_PERM:C_PERM + P] = p[:, None] == (p[None, :] ^ 32)
    q, rp = p % GRID_W, p // GRID_W
    start = np.clip(q - WIN_COLS // 2, 0, GRID_W - WIN_COLS)
    k = np.arange(GRID_W)
    inside = (k[None] >= start[:, None]) & (k[None] < start[:, None] + WIN_COLS)
    c[:, C_EDGE:C_EDGE + GRID_W] = np.where(inside, 0, NEG)
    j = np.arange(INTR)
    rows = (j[None] >= rp[:, None]) & (j[None] < rp[:, None] + WIN_ROWS)
    c[:, C_INT:C_P4] = np.where(rows[:, :, None] & inside[:, None, :], 0, NEG).reshape(P, -1)
    c[:, C_P4:C_P16] = NG - np.arange(NG)
    c[:, C_P16:C_THR] = NE - np.arange(NE)
    c[:, C_THR:C_IOTA] = 1 + np.arange(16)
    c[:, C_IOTA:C_HALF] = np.arange(64)
    c[:, C_HALF:] = -0.5
    t = np.arange(SEQ)
    freq = np.float32(10000.0) ** (-np.arange(16, dtype=np.float32) / 16)
    ang = np.concatenate([(t // GRID_W).astype(np.float32)[:, None] * freq,
                          (t % GRID_W).astype(np.float32)[:, None] * freq], axis=-1)
    cos, sin = np.cos(ang).T, np.sin(ang).T
    trig = np.concatenate([np.tile(cos, (4, 1)), np.concatenate([-sin, sin, -sin, sin])], axis=1)
    tok = np.broadcast_to((np.arange(NT)[None, :] * P + p[:, None])[:, :, None], (P, NT, 16))
    return c, np.ascontiguousarray(trig, np.float32), np.ascontiguousarray(tok, np.int32)


class Steps:

    def __init__(self, eng, sem, base=0):
        self.eng, self.sem, self.base, self.n = eng, sem, base, 0

    def then(self, ins):
        ins.then_inc(self.sem, 1)
        self.n += 1
        self.eng.wait_ge(self.sem, self.base + self.n)


def window(t):
    if t >= LT:
        return 0, 0
    return (t - 2, 5) if 2 <= t < 6 else (0, 4) if t < 2 else (4, 4)


def build(nc, a):
    out = a["out"]
    dram = lambda name, shape, dt=F32: nc.dram_tensor(name, shape, dt, kind="Internal").ap()
    mods = dram("mods", [2, 2, NMOD * D])
    toep = dram("toep", [16, GRID_W, 15, GRID_W])
    h_dram = dram("h_rows", [NTOK, D])
    idx_dram = [dram(f"slot_token{l}", [(ITEMS[l] + 1) * CAP[l], 16], I32) for l in range(2)]
    ys = dram("slot_out", [max(ITEMS[l] * CAP[l] for l in range(2)), D])

    top = ExitStack()

    seen = {}

    def unique(name):
        seen[name] = seen.get(name, 0) + 1
        return name if seen[name] == 1 else f"{name}_{seen[name]}"

    def sb(c, name, shape, dt=F32):
        return c.enter_context(nc.sbuf_tensor(unique(name), shape, dt))

    stage_sems = []
    software = {"idx_cleared", "slots_cleared", "rt_scattered", "idx_in", "x_gathered", "y_in0", "y_in1", "y_in2"}

    def sem(c, name):
        handle = nc.alloc_semaphore(name=unique(name))
        if name not in software:
            stage_sems.append(handle)
        return handle

    with top:
        x = sb(top, "x_res", [P, NT, D])
        con = sb(top, "con", [P, C_ALL])
        rows = sb(top, "rows", [P, 4, D])
        ss = sb(top, "ss", [P, NT])
        std = sb(top, "std", [P, NT])
        rstd = sb(top, "rstd", [P, NT])
        slots = sb(top, "slots", [P, NT, 2], I32)
        gates = sb(top, "gates", [P, NT, 2])
        table = sb(top, "table", [P, 64], I32)
        nitem = sb(top, "nitem", [P, 1], I32)
        ps = top.enter_context(nc.psum_tensor("ps", [P, 8 * HALF], F32))
        bank = lambda n, c0=0, c1=HALF: ps[:, n * HALF + c0:n * HALF + c1]
        ident = con[:, C_ID:C_ID + P]

        def modulation():
            with ExitStack() as c:
                cc = sb(c, "cc", [P, 2, KD])
                cact = sb(c, "cact", [P, 2, KD])
                modr = sb(c, "modr", [2, 2, NMOD * D])
                gn = sb(c, "gn", [2, 2, 2, D])
                W = sb(c, "mod_ring", [P, 4, KD, HALF])
                zero = sb(c, "zero", [P, 1024], I32)
                NP = NMOD * D // HALF
                s_c, s_x, s_b, s_con, s_toep = (sem(c, n) for n in ("c_in", "x_in", "bias_in", "con_in", "toep_out"))
                w_in = [sem(c, f"modw_in{n}") for n in range(4)]
                s_act, s_mm, s_add, s_rows, s_out = (sem(c, n) for n in ("silu_done", "mod_mm", "mod_add", "mod_rows", "mod_out"))
                s_zero, s_idx = sem(c, "zero_set"), sem(c, "idx_cleared")
                block = c.enter_context(nc.Block())

                @block.sync
                def _(sp):
                    sp.dma_start(cc[:, 0, :], a["c"].rearrange("b (p k) -> p (b k)", k=KD)).then_inc(s_c, 16)
                    sp.dma_start(cc[:, 1, :], a["c_ctx"].rearrange("(p k) -> p k", k=KD)).then_inc(s_c, 16)
                    for l in range(2):
                        src = a["mod_w"][l].rearrange("(p k) n -> p k n", k=KD)
                        with sp.Fori(0, NP // 4) as it:
                            for s in range(4):
                                sp.wait_ge(s_mm, it * 4 + l * NP + s + 1)
                                sp.dma_start(W[:, s], src[:, :, bass.ds((it * 4 + s) * HALF, HALF)]).then_inc(w_in[s], 16)
                    for l in range(2):
                        sp.wait_ge(s_rows, 2 * l + 2)
                        sp.dma_start(mods[l], modr[:, l, :]).then_inc(s_out, 16)
                    sp.wait_ge(s_out, 32)

                @block.scalar
                def _(act):
                    act.dma_start(con[:, :], a["consts"]).then_inc(s_con, 16)
                    for l in range(2):
                        act.dma_start(modr[:, l, :], a["mod_b"][l].partition_broadcast(2)).then_inc(s_b, 16)
                        act.dma_start(gn[:, l, 0, :], a["norm_mix"][l].partition_broadcast(2)).then_inc(s_b, 16)
                        act.dma_start(gn[:, l, 1, :], a["norm_ffn"][l].partition_broadcast(2)).then_inc(s_b, 16)
                    act.wait_ge(s_c, 32)
                    nc.scalar.activation(cact[:, :, :], cc[:, :, :], ACT.Silu).then_inc(s_act, 1)
                    act.dma_start(x[:, 0:LT, :], a["x"][0].rearrange("(t p) d -> p t d", p=P)).then_inc(s_x, 16)
                    act.dma_start(x[:, LT:NT, :], a["ctx"][0].rearrange("(t p) d -> p t d", p=P)).then_inc(s_x, 16)
                    for h in range(16):
                        src = a["rpb_pad"][h]
                        src = bass.AP(src.tensor, src.offset + GRID_W - 1, [[P, 15], [-1, GRID_W], [1, GRID_W]])
                        act.dma_start(toep[h].rearrange("q r k -> r q k"), src).then_inc(s_toep, 16)
                    act.wait_ge(s_x, 32)
                    act.wait_ge(s_con, 16)
                    act.wait_ge(s_toep, 256)

                @block.tensor
                def _(pe):
                    pe.wait_ge(s_act, 1)
                    pe.sem_inc(s_mm, 4)
                    for l in range(2):
                        with pe.Fori(0, NP // 4) as it:
                            for s in range(4):
                                pe.wait_ge(w_in[s], (it + l * (NP // 4) + 1) * 16)
                                pe.wait_ge(s_add, it * 4 + l * NP + s + 1)
                                for k in range(KD):
                                    m = nc.tensor.matmul(bank(s)[0:2, :], cact[:, :, k], W[:, s, k, :],
                                                         start=k == 0, stop=k == KD - 1)
                                m.then_inc(s_mm, 1)

                @block.vector
                def _(dve):
                    dve.wait_ge(s_b, 96)
                    dve.sem_inc(s_add, 4)
                    for l in range(2):
                        with dve.Fori(0, NP // 4) as it:
                            for s in range(4):
                                dve.wait_ge(s_mm, it * 4 + l * NP + s + 5)
                                cols = bass.ds((it * 4 + s) * HALF + l * NMOD * D, HALF)
                                flat = modr[:, :, :].rearrange("v l n -> v (l n)")
                                nc.vector.tensor_tensor(flat[:, cols], bank(s)[0:2, :], flat[:, cols],
                                                        ALU.add).then_inc(s_add, 1)
                    for l in range(2):
                        for n, r in enumerate((1, 4)):
                            dve.wait_ge(s_add, 4 + NP * 2)
                            v = modr[:, l, r * D:(r + 1) * D]
                            nc.vector.scalar_tensor_tensor(out=v, in0=v, scalar=1.0, in1=gn[:, l, n, :],
                                                           op0=ALU.add, op1=ALU.mult).then_inc(s_rows, 1)

                @block.gpsimd
                def _(pool):
                    nc.gpsimd.memset(zero[:, :], 0).then_inc(s_zero, 1)
                    pool.wait_ge(s_zero, 1)
                    for l in range(2):
                        flat = idx_dram[l].rearrange("s n -> (s n)")
                        total = (ITEMS[l] + 1) * CAP[l] * 16
                        per = total // P
                        pool.dma_start(flat.rearrange("(p n) -> p n", p=P), zero[:, 0:per]).then_inc(s_idx, 16)
                    pool.wait_ge(s_idx, 32)

        def normed(l, ffn, hT, rw=None):
            T = NT if (l == 0 or not ffn) else LT
            with ExitStack() as c:
                junk = sb(c, "junk", [P, D])
                hr = sb(c, "hr", [P, 3, D])
                s_rows, s_ss, s_rstd, s_sc, s_h = (sem(c, n) for n in (
                    "rows_in", "ss_done", "rstd_done", "h_scaled", "h_ready"))
                s_tr, s_eva, s_evd, s_rt, s_rw = (sem(c, n) for n in (
                    "h_transposed", "hT_low", "hT_high", "routed", "router_in"))
                s_st = [sem(c, f"h_stored{n}") for n in range(3)]
                block = c.enter_context(nc.Block())
                B, A = (3, 4) if ffn else (0, 1)

                @block.sync
                def _(sp):
                    for v in range(2 if T > LT else 1):
                        for n, r in enumerate((A, B)):
                            sp.dma_start(rows[:, 2 * v + n, :], mods[l, v, r * D:(r + 1) * D].partition_broadcast(P)).then_inc(s_rows, 16)
                    if ffn:
                        sp.dma_start(rw[:, :, :], a["router_w"].rearrange("(k p) e -> p k e", p=P)).then_inc(s_rw, 16)
                        for t in range(T):
                            sp.wait_ge(s_h, t + 1)
                            sp.dma_start(h_dram[t * P:(t + 1) * P, :], hr[:, t % 3, :]).then_inc(s_st[t % 3], 16)
                        for n in range(3):
                            sp.wait_ge(s_st[n], 16 * len(range(n, T, 3)))

                @block.scalar
                def _(act):
                    for t in range(T):
                        if t:
                            act.wait_ge(s_ss, t)
                        nc.scalar.activation(junk[:, :], x[:, t, :], ACT.Square, accum_out=ss[:, t:t + 1]).then_inc(s_ss, 1)
                    for t in range(T):
                        act.wait_ge(s_tr, 2 * t + 1)
                        nc.scalar.activation(hT[:, 0:4, t * P:(t + 1) * P], bank(2 * (t % 2)).rearrange("p (k n) -> p k n", n=P),
                                             ACT.Copy).then_inc(s_eva, 1)

                def high(dve, t):
                    dve.wait_ge(s_tr, 2 * t + 2)
                    nc.vector.tensor_copy(hT[:, 4:8, t * P:(t + 1) * P],
                                          bank(2 * (t % 2) + 1).rearrange("p (k n) -> p k n", n=P)).then_inc(s_evd, 1)

                @block.vector
                def _(dve):
                    dve.wait_ge(s_ss, T)
                    nc.vector.tensor_scalar(std[:, 0:T], ss[:, 0:T], 1.0 / D, EPS, ALU.mult, ALU.add).then_inc(s_rstd, 1)
                    dve.wait_ge(s_rstd, 2)
                    dve.wait_ge(s_rows, 64 if T > LT else 32)
                    for t in range(T):
                        if t >= 3:
                            dve.wait_ge(s_tr, 2 * (t - 3) + 2)
                            if ffn:
                                dve.wait_ge(s_st[t % 3], 16 * (t // 3))
                        v = 2 * (t >= LT)
                        nc.vector.scalar_tensor_tensor(out=hr[:, t % 3, :], in0=x[:, t, :], scalar=rstd[:, t:t + 1],
                                                       in1=rows[:, v, :], op0=ALU.mult, op1=ALU.mult).then_inc(s_sc, 1)
                        if t:
                            high(dve, t - 1)
                    high(dve, T - 1)

                @block.gpsimd
                def _(pool):
                    pool.wait_ge(s_rstd, 1)
                    nc.gpsimd.tensor_tensor(rstd[:, 0:T], std[:, 0:T], con[:, C_HALF:C_HALF + T], ALU.pow).then_inc(s_rstd, 1)
                    pool.wait_ge(s_rows, 64 if T > LT else 32)
                    for t in range(T):
                        pool.wait_ge(s_sc, t + 1)
                        v = 2 * (t >= LT)
                        nc.gpsimd.tensor_tensor(hr[:, t % 3, :], hr[:, t % 3, :], rows[:, v + 1, :], ALU.add).then_inc(s_h, 1)

                def route(pe, t):
                    pe.wait_ge(s_eva, t + 1)
                    pe.wait_ge(s_evd, t + 1)
                    for k in range(KD):
                        m = nc.tensor.matmul(bank(7, t * NE, (t + 1) * NE), hT[:, k, t * P:(t + 1) * P], rw[:, k, :],
                                             start=k == 0, stop=k == KD - 1)
                    m.then_inc(s_rt, 1)

                @block.tensor
                def _(pe):
                    if ffn:
                        pe.wait_ge(s_rw, 16)
                    for t in range(T):
                        pe.wait_ge(s_h, t + 1)
                        if t >= 2:
                            pe.wait_ge(s_eva, t - 1)
                            pe.wait_ge(s_evd, t - 1)
                        for k in range(KD):
                            b = 2 * (t % 2) + k // 4
                            m = nc.tensor.transpose(bank(b, (k % 4) * P, (k % 4 + 1) * P), hr[:, t % 3, k * P:(k + 1) * P], ident)
                            if k % 4 == 3:
                                m.then_inc(s_tr, 1)
                        if ffn and t:
                            route(pe, t - 1)
                    if ffn:
                        route(pe, T - 1)

        def load_output_weights(sp, l, hT, wo_in):
            wo = a["w_o"][l].rearrange("(k p) n -> p k n", p=P)
            for k in range(0, KD, 2):
                sp.dma_start(hT[:, k:k + 2, 0:D], wo[:, k:k + 2, :]).then_inc(wo_in, 16)
            for v in range(2 if l == 0 else 1):
                sp.dma_start(rows[:, 3 - v, :], mods[l, v, 2 * D:3 * D].partition_broadcast(P)).then_inc(wo_in, 16)

        def neighbourhood(hT, oT, wo_in):
            with ExitStack() as c:
                wq = sb(c, "na_wqkv", [P, 3, KD, P])
                qT = sb(c, "na_qT", [P, NTOK])
                kT = sb(c, "na_kT", [P, NTOK])
                V = sb(c, "na_V", [P, NT, P])
                pb = sb(c, "na_probs", [P, 3, 7 * P])
                pT = sb(c, "na_probsT", [P, 2, 7 * P])
                osb = sb(c, "na_out", [P, 2, P])
                mx = sb(c, "na_negmax", [P, 4])
                ls = sb(c, "na_sum", [P, 4])
                rl = sb(c, "na_suminv", [P, 2])
                raw = sb(c, "bias_raw", [P, 2, TABR * GRID_W])
                tin = sb(c, "bias_interior", [P, 2, INTR * GRID_W])
                ted = sb(c, "bias_edge", [P, 2, TABR * GRID_W])
                zeros = rows[:, 0, 0:HALF]
                s_z, s_cleared = sem(c, "zeros_set"), sem(c, "slots_cleared")
                w_in, s_mm, s_qk, s_v, s_S, s_pre, s_max, s_exp, s_T, s_pT, s_o, s_rl, s_osb, s_oTp, s_oT, s_raw, s_tab = (
                    sem(c, n) for n in ("na_w_in", "na_projected", "na_qk_taken", "na_v_taken", "na_scores", "na_biased",
                                        "na_max", "na_exp", "na_transposed", "na_probsT_ready", "na_pv", "na_inverse",
                                        "na_out_taken", "na_outT_psum", "na_outT", "na_bias_in", "na_bias_table"))
                block = c.enter_context(nc.Block())
                steps = [(t, h) for t in range(NT) for h in range(2)]
                NS = len(steps)
                chunks = [("q", 0, 512), ("q", 512, 512), ("q", 1024, 256), ("k", 0, 512), ("k", 512, 512), ("k", 1024, 256),
                          ("v", 0, 4), ("v", 4, 4), ("v", 8, 2)]
                NM, NQK = len(chunks), 6

                def keys(s):
                    k0, n = window(steps[s][0])
                    return list(range(k0, k0 + n)) + list(range(LT, NT))

                def parts(s):
                    k0, n = window(steps[s][0])
                    return {0: [(0, 256, SEQ)], 4: [(0, 512, k0 * P), (512, 256, SEQ)],
                            5: [(0, 512, k0 * P), (512, 128, (k0 + 4) * P), (640, 256, SEQ)]}[n]

                def rounds(s):
                    n = len(keys(s))
                    return [(0, min(n, 4))] + ([(4, n)] if n > 4 else [])

                rb = np.cumsum([0] + [len(rounds(s)) for s in range(NS)]).tolist()
                NR = rb[-1]
                S = lambda s, c0, c1: ps[:, (s % 2) * 2 * HALF + c0:(s % 2) * 2 * HALF + c1]
                O = lambda s: bank(4 if s % 2 == 0 else 7, 0, HD)
                OT = bank(6, 384, 512)

                @block.sync
                def _(sp):
                    src = a["w_qkv"][0].rearrange("(k p) n -> p k n", p=P)
                    tv = toep.rearrange("h q r k -> (h q) (r k)")
                    with sp.Fori(0, GROUPS) as g:
                        sp.wait_ge(s_mm, g * NM + 1)
                        for j in range(3):
                            sp.dma_start(wq[:, j], src[:, :, bass.ds(g * P + j * D, P)]).then_inc(w_in, 16)
                        sp.wait_ge(s_tab, g * 4 + 1)
                        for h in range(2):
                            for r in range(2):
                                sp.dma_start(raw[r * GRID_W:(r + 1) * GRID_W, h, :],
                                             tv[bass.ds((g * 2 + h) * GRID_W, GRID_W), (1 - r) * GRID_W:(1 - r + TABR) * GRID_W]).then_inc(s_raw, 16)
                    sp.wait_ge(s_mm, GROUPS * NM + 1)
                    load_output_weights(sp, 0, hT, wo_in)

                @block.gpsimd
                def _(pool):
                    pool.sem_inc(s_tab, 1)
                    nc.gpsimd.memset(zeros, 0.0).then_inc(s_z, 1)
                    pool.wait_ge(s_z, 1)
                    rest = ys.rearrange("(p n) (b d) -> p (n b) d", p=P, d=HALF)
                    for n in range(0, rest.shape[1], 16):
                        m = min(16, rest.shape[1] - n)
                        pool.dma_start(rest[:, n:n + m, :], zeros.unsqueeze(1).to_broadcast([P, m, HALF])).then_inc(s_cleared, 16)
                    pool.wait_ge(s_cleared, 16 * -(-rest.shape[1] // 16))
                    with pool.Fori(0, GROUPS) as g:
                        pool.wait_ge(s_raw, (g + 1) * 64)
                        pool.wait_ge(s_pre, g * NS + 1)
                        for h in range(2):
                            v = lambda z, j0, j1: z[:, h, j0 * GRID_W:j1 * GRID_W].rearrange("p (j k) -> p j k", k=GRID_W)
                            nc.gpsimd.tensor_tensor(v(ted, 0, TABR), v(raw, 0, TABR),
                                                    con[:, C_EDGE:C_INT].unsqueeze(1).to_broadcast([P, TABR, GRID_W]), ALU.add).then_inc(s_tab, 1)
                            nc.gpsimd.tensor_tensor(tin[:, h, :], raw[:, h, 2 * GRID_W:(2 + INTR) * GRID_W],
                                                    con[:, C_INT:C_P4], ALU.add).then_inc(s_tab, 1)

                @block.tensor
                def _(pe):
                    pe.sem_inc(s_mm, 1)
                    with pe.Fori(0, GROUPS) as g:
                        pe.wait_ge(w_in, (g + 1) * 48)
                        for n, (kind, c0, w) in enumerate(chunks):
                            if n >= 4:
                                pe.wait_ge(s_qk, g * NQK + n - 3)
                            b = n % 4
                            if kind == "v":
                                for t in range(w):
                                    for k in range(KD):
                                        m = nc.tensor.matmul(bank(b, t * P, (t + 1) * P), hT[:, k, (c0 + t) * P:(c0 + t + 1) * P],
                                                             wq[:, 2, k, :], start=k == 0, stop=k == KD - 1)
                            else:
                                for k in range(KD):
                                    m = nc.tensor.matmul(bank(b, 0, w), wq[:, 0 if kind == "q" else 1, k, :],
                                                         hT[:, k, c0:c0 + w], start=k == 0, stop=k == KD - 1)
                            m.then_inc(s_mm, 1)
                        pe.wait_ge(s_qk, g * NQK + NQK)
                        pe.wait_ge(s_v, g * 3 + 3)

                        def scores(s):
                            t, h = steps[s]
                            r = slice(h * HD, (h + 1) * HD)
                            if s >= 2:
                                pe.wait_ge(s_pre, g * NS + s)
                            for c0, w, k0 in parts(s):
                                m = nc.tensor.matmul(S(s, c0, c0 + w), qT[r, t * P:(t + 1) * P], kT[r, k0:k0 + w], start=True, stop=True)
                            m.then_inc(s_S, 1)

                        def out_transpose(t):
                            pe.wait_ge(s_osb, g * NS + 2 * t + 2)
                            nc.tensor.transpose(OT, osb[:, t % 2, :], ident).then_inc(s_oTp, 1)

                        scores(0)
                        scores(1)
                        for s in range(NS):
                            t, h = steps[s]
                            pe.wait_ge(s_exp, g * NS + s + 1)
                            for r, (i0, i1) in enumerate(rounds(s)):
                                if r and h == 0 and t >= 2:
                                    pe.wait_ge(s_oT, g * NT + t - 1)
                                for i in range(i0, i1):
                                    m = nc.tensor.transpose(bank(5 + r, (i - i0) * P, (i - i0 + 1) * P), pb[:, s % 3, i * P:(i + 1) * P], ident)
                                m.then_inc(s_T, 1)
                            if h == 1 and t:
                                if not rounds(s)[1:]:
                                    pe.wait_ge(s_oT, g * NT + t - 1)
                                out_transpose(t - 1)
                            if s + 2 < NS:
                                scores(s + 2)
                            pe.wait_ge(s_pT, g * NR + rb[s + 1])
                            if s >= 2:
                                pe.wait_ge(s_osb, g * NS + s - 1)
                            ks = keys(s)
                            for i, kt in enumerate(ks):
                                m = nc.tensor.matmul(O(s), pT[:, s % 2, i * P:(i + 1) * P], V[:, kt, h * HD:(h + 1) * HD],
                                                     start=i == 0, stop=i == len(ks) - 1)
                            m.then_inc(s_o, 1)
                        pe.wait_ge(s_oT, g * NT + NT - 1)
                        out_transpose(NT - 1)

                @block.vector
                def _(dve):
                    dve.sem_inc(s_pre, 1)
                    with dve.Fori(0, GROUPS) as g:
                        for n in range(3):
                            kind, t0, w = chunks[NQK + n]
                            dve.wait_ge(s_mm, g * NM + NQK + n + 2)
                            nc.vector.tensor_copy(V[:, t0:t0 + w, :], bank((NQK + n) % 4, 0, w * P).rearrange("p (t n) -> p t n", n=P)).then_inc(s_v, 1)
                        dve.wait_ge(s_tab, (g + 1) * 4 + 1)

                        def soft(s):
                            t, h = steps[s]
                            k0, n = window(t)
                            dve.wait_ge(s_S, g * NS + s + 1)
                            if s >= 3:
                                dve.wait_ge(s_T, g * NR + rb[s - 2])
                            w = n * P
                            if n:
                                j0 = 2 * k0 - 2 * t + 6
                                bias = tin[:, h, :] if n == 5 else ted[:, h, j0 * GRID_W:(j0 + WIN_ROWS) * GRID_W]
                                nc.vector.tensor_tensor(pb[:, s % 3, 0:w], S(s, 0, w), bias, ALU.add).then_inc(s_rl, 1)
                            else:
                                dve.sem_inc(s_rl, 1)
                            nc.vector.tensor_copy(pb[:, s % 3, w:w + CTX], S(s, w, w + CTX)).then_inc(s_pre, 1)
                            dve.wait_ge(s_rl, g * 2 * NS + rln(s))
                            dve.wait_ge(s_pre, g * NS + s + 2)
                            nc.vector.tensor_reduce(mx[:, s % 4:s % 4 + 1], pb[:, s % 3, 0:w + CTX], AX.X, ALU.max, negate=True).then_inc(s_max, 1)

                        def rln(s):
                            return s + 1 + max(0, s - 2)

                        def take(s):
                            t, h = steps[s]
                            dve.wait_ge(s_o, g * NS + s + 1)
                            nc.vector.reciprocal(rl[:, s % 2:s % 2 + 1], ls[:, s % 4:s % 4 + 1]).then_inc(s_rl, 1)
                            dve.wait_ge(s_rl, g * 2 * NS + min(s + 3, NS) + s + 1)
                            if h == 0 and t >= 2:
                                dve.wait_ge(s_oTp, g * NT + t - 1)
                            nc.vector.tensor_scalar(osb[:, t % 2, h * HD:(h + 1) * HD], O(s), rl[:, s % 2:s % 2 + 1], None, ALU.mult).then_inc(s_osb, 1)

                        soft(0)
                        soft(1)
                        for s in range(NS):
                            if s + 2 < NS:
                                soft(s + 2)
                            take(s)

                @block.scalar
                def _(act):
                    with act.Fori(0, GROUPS) as g:
                        for n in range(NQK):
                            kind, c0, w = chunks[n]
                            act.wait_ge(s_mm, g * NM + n + 2)
                            nc.scalar.activation((qT if kind == "q" else kT)[:, c0:c0 + w], bank(n % 4, 0, w), ACT.Copy,
                                                 scale=SCALE if kind == "q" else 1.0).then_inc(s_qk, 1)

                        def exp(s):
                            w = len(keys(s)) * P
                            act.wait_ge(s_max, g * NS + s + 1)
                            nc.scalar.activation(pb[:, s % 3, 0:w], pb[:, s % 3, 0:w], ACT.Exp, bias=mx[:, s % 4:s % 4 + 1],
                                                 accum_out=ls[:, s % 4:s % 4 + 1]).then_inc(s_exp, 1)

                        def outT(t):
                            act.wait_ge(s_oTp, g * NT + t + 1)
                            nc.scalar.activation(oT[:, bass.ds(g * NTOK + t * P, P)], OT, ACT.Copy).then_inc(s_oT, 1)

                        exp(0)
                        for s in range(NS):
                            t, h = steps[s]
                            for r, (i0, i1) in enumerate(rounds(s)):
                                act.wait_ge(s_T, g * NR + rb[s] + r + 1)
                                if r and h == 1 and t:
                                    act.wait_ge(s_oTp, g * NT + t)
                                nc.scalar.activation(pT[:, s % 2, i0 * P:i1 * P], bank(5 + r, 0, (i1 - i0) * P), ACT.Copy).then_inc(s_pT, 1)
                            if h == 1 and t:
                                outT(t - 1)
                            if s + 1 < NS:
                                exp(s + 1)
                        outT(NT - 1)

        def differential(hT, oT, wo_in):
            with ExitStack() as c:
                wq = sb(c, "df_wqkv", [P, 3, KD, P])
                qT = sb(c, "df_qT", [P, SEQ])
                kT = sb(c, "df_kT", [P, NTOK])
                V = sb(c, "df_V", [P, NT, P])
                rq = sb(c, "df_raw_qk", [P, 2, SEQ])
                trig = sb(c, "trig", [P, 2, SEQ])
                pb = sb(c, "df_probs", [P, 3, NTOK])
                pT = rows[:, :, :].rearrange("p r d -> p (r d)")[:, 0:2 * NTOK].rearrange("p (b n) -> p b n", b=2)
                mx = sb(c, "df_negmax", [P, 4])
                ls = sb(c, "df_sum", [P, 4])
                rl = sb(c, "df_suminv", [P, 4])
                cf = sb(c, "df_weight", [P, 2])
                lam = sb(c, "lam", [P, 4, HD])
                lamt = sb(c, "lamt", [P, 2, HD])
                lams = sb(c, "lams", [P, 6])
                gsub = sb(c, "gsub", [P, 1])
                oraw = sb(c, "df_out", [P, 2, P])
                osq = sb(c, "df_square", [P, P])
                oss = sb(c, "df_sumsq", [P, 3])
                osb = sb(c, "df_normed", [P, 2, P])
                w_in, s_mm, s_qk, s_v, s_S, s_max, s_exp, s_T, s_pT, s_o, s_cf, s_dif, s_on, s_osb, s_oTp, s_oT, s_rop, s_sin, s_cos, s_rot, s_lin, s_lam, s_half = (
                    sem(c, n) for n in ("df_w_in", "df_projected", "df_qk_taken", "df_v_taken", "df_scores", "df_max", "df_exp",
                                        "df_transposed", "df_probsT_ready", "df_pv", "df_weight_steps", "df_combined", "df_norm_steps",
                                        "df_out_ready", "df_outT_psum", "df_outT", "df_partner", "df_sin", "df_cos", "df_rotated",
                                        "df_consts_in", "lambda_steps", "df_map0_scored"))
                block = c.enter_context(nc.Block())
                chunks = [("q", 0, 512), ("q", 512, 512), ("k", 0, 512), ("k", 512, 512), ("k", 1024, 256),
                          ("v", 0, 4), ("v", 4, 4), ("v", 8, 2)]
                NM, NQK, NROT = len(chunks), 5, 4
                parts = (((0, 0, 512), (512, 512, 512), (SEQ, SEQ, CTX)),
                         ((NTOK, SEQ, CTX), (NTOK + CTX, 0, 512), (NTOK + CTX + 512, 512, 512)))
                S = lambda m: ps[:, m * NTOK:(m + 1) * NTOK]
                rounds = ((0, 4), (4, 8), (8, NT))
                NR = len(rounds)
                TB = lambda r: 5 + r % 2
                O = bank(7, 0, P)
                OT = bank(6, 0, P)
                rot = lambda r: (r // 2, slice((r % 2) * 512, (r % 2) * 512 + 512))

                @block.sync
                def _(sp):
                    sp.dma_start(trig[:, :, :], a["trig"].rearrange("p (a n) -> p a n", a=2)).then_inc(s_lin, 16)
                    sp.dma_start(lam[:, :, :], a["diff_lambda"][0].rearrange("a d -> (a d)").partition_broadcast(P)
                                 .rearrange("p (a d) -> p a d", a=4)).then_inc(s_lin, 16)
                    sp.dma_start(gsub[:, :], a["diff_subln"][0].rearrange("(p a) -> p a", a=1)).then_inc(s_lin, 16)
                    src = a["w_qkv"][1].rearrange("(k p) n -> p k n", p=P)
                    with sp.Fori(0, GROUPS) as g:
                        sp.wait_ge(s_mm, g * NM + 1)
                        for j in range(3):
                            sp.dma_start(wq[:, j], src[:, :, bass.ds(g * P + j * D, P)]).then_inc(w_in, 16)
                    sp.wait_ge(s_mm, GROUPS * NM + 1)
                    load_output_weights(sp, 1, hT, wo_in)

                @block.gpsimd
                def _(pool):
                    pool.wait_ge(s_lin, 48)
                    with pool.Fori(0, GROUPS) as g:
                        for r in range(NROT):
                            i, cols = rot(r)
                            pool.wait_ge(s_rop, g * NROT + r + 1)
                            nc.gpsimd.tensor_tensor(rq[:, i, cols], rq[:, i, cols], trig[:, 0, cols], ALU.mult).then_inc(s_cos, 1)
                        for t in range(LT):
                            pool.wait_ge(s_on, g * 4 * LT + 4 * t + 3)
                            nc.gpsimd.tensor_tensor(oss[:, 2:3], oss[:, 1:2], con[:, C_HALF:C_HALF + 1], ALU.pow).then_inc(s_on, 1)

                @block.tensor
                def _(pe):
                    pe.sem_inc(s_mm, 1)
                    with pe.Fori(0, GROUPS) as g:
                        pe.wait_ge(w_in, (g + 1) * 48)
                        for n, (kind, c0, w) in enumerate(chunks):
                            if n >= 6:
                                pe.wait_ge(s_qk, g * NQK + n - 5)
                            if kind == "v":
                                for t in range(w):
                                    for k in range(KD):
                                        m = nc.tensor.matmul(bank(n % 6, t * P, (t + 1) * P), hT[:, k, (c0 + t) * P:(c0 + t + 1) * P],
                                                             wq[:, 2, k, :], start=k == 0, stop=k == KD - 1)
                            else:
                                for k in range(KD):
                                    m = nc.tensor.matmul(bank(n % 6, 0, w), wq[:, 0 if kind == "q" else 1, k, :],
                                                         hT[:, k, c0:c0 + w], start=k == 0, stop=k == KD - 1)
                            m.then_inc(s_mm, 1)
                        for r in range(NROT):
                            i, cols = rot(r)
                            pe.wait_ge(s_qk, g * NQK + (r + 3 if r < 3 else NQK))
                            nc.tensor.matmul(bank((2, 3, 4, 6)[r]), con[:, C_PERM:C_PERM + P], rq[:, i, cols],
                                             start=True, stop=True).then_inc(s_rop, 1)
                        pe.wait_ge(s_v, g * 3 + 3)
                        pe.wait_ge(s_rot, g * NROT + NROT)

                        def scores(t, m, which):
                            r = slice(m * HD, (m + 1) * HD)
                            for n in which:
                                c0, k0, w = parts[m][n]
                                mm = nc.tensor.matmul(ps[:, c0:c0 + w], qT[r, t * P:(t + 1) * P], kT[r, k0:k0 + w], start=True, stop=True)
                            return mm

                        def scores_first(t):
                            if t:
                                pe.wait_ge(s_exp, g * 2 * LT + 2 * t - 1)
                            scores(t, 0, (0, 1))

                        def scores_rest(t):
                            if t:
                                pe.wait_ge(s_exp, g * 2 * LT + 2 * t)
                            scores(t, 0, (2,)).then_inc(s_half, 1)
                            scores(t, 1, (1,))
                            pe.wait_ge(s_half, g * LT + t + 1)
                            scores(t, 1, (0,)).then_inc(s_S, 1)
                            scores(t, 1, (2,)).then_inc(s_S, 1)

                        def transposes(t, r):
                            if r == 1 and t >= 2:
                                pe.wait_ge(s_oT, g * LT + t - 1)
                            if r == 2:
                                pe.wait_ge(s_pT, g * LT * NR + t * NR + 1)
                            i0, i1 = rounds[r]
                            for i in range(i0, i1):
                                mm = nc.tensor.transpose(bank(TB(r), (i - i0) * P, (i - i0 + 1) * P), pb[:, t % 2, i * P:(i + 1) * P], ident)
                            mm.then_inc(s_T, 1)

                        def pv(t, r):
                            pe.wait_ge(s_pT, g * LT * NR + t * NR + r + 1)
                            if r == 0 and t:
                                pe.wait_ge(s_on, g * 4 * LT + 4 * t - 3)
                            for i in range(*rounds[r]):
                                mm = nc.tensor.matmul(O, pT[:, t % 2, i * P:(i + 1) * P], V[:, i, :], start=i == 0, stop=i == NT - 1)
                            if r == NR - 1:
                                mm.then_inc(s_o, 1)

                        def out_transpose(t):
                            pe.wait_ge(s_osb, g * LT + t + 1)
                            if t == LT - 1:
                                pe.wait_ge(s_oT, g * LT + t)
                            nc.tensor.transpose(OT, osb[:, t % 2, :], ident).then_inc(s_oTp, 1)

                        for t in range(2):
                            scores_first(t)
                            scores_rest(t)
                        for t in range(LT):
                            pe.wait_ge(s_dif, g * LT + t + 1)
                            transposes(t, 0)
                            transposes(t, 1)
                            pv(t, 0)
                            transposes(t, 2)
                            pv(t, 1)
                            pv(t, 2)
                            if t + 2 < LT:
                                scores_first(t + 2)
                                scores_rest(t + 2)
                            if t:
                                out_transpose(t - 1)
                        out_transpose(LT - 1)

                @block.scalar
                def _(act):
                    act.wait_ge(s_lam, 2)
                    nc.scalar.activation(lams[:, 2:4], lams[:, 0:2], ACT.Exp).then_inc(s_lam, 1)
                    with act.Fori(0, GROUPS) as g:
                        for n in range(NQK):
                            kind, c0, w = chunks[n]
                            act.wait_ge(s_mm, g * NM + n + 2)
                            dst = kT[:, c0:c0 + w] if c0 >= SEQ else rq[:, 0 if kind == "q" else 1, c0:c0 + w]
                            nc.scalar.activation(dst, bank(n, 0, w), ACT.Copy, scale=SCALE if kind == "q" else 1.0).then_inc(s_qk, 1)

                        def exp(t, m):
                            act.wait_ge(s_max, g * 2 * LT + 2 * t + 2)
                            if m == 1 and t:
                                act.wait_ge(s_dif, g * LT + t)
                            if m == 0 and t >= 2:
                                act.wait_ge(s_T, g * LT * NR + (t - 1) * NR)
                            nc.scalar.activation(pb[:, t % 2 if m == 0 else 2, :], S(m), ACT.Exp,
                                                 bias=mx[:, 2 * (t % 2) + m:2 * (t % 2) + m + 1],
                                                 accum_out=ls[:, 2 * (t % 2) + m:2 * (t % 2) + m + 1]).then_inc(s_exp, 1)

                        def outT(t):
                            act.wait_ge(s_oTp, g * LT + t + 1)
                            act.wait_ge(s_lam, 6)
                            nc.scalar.activation(oT[:, bass.ds(g * NTOK + t * P, P)], OT, ACT.Copy, scale=gsub[:, 0:1]).then_inc(s_oT, 1)

                        def take_probs(t, r):
                            i0, i1 = rounds[r]
                            act.wait_ge(s_T, g * LT * NR + t * NR + r + 1)
                            nc.scalar.activation(pT[:, t % 2, i0 * P:i1 * P], bank(TB(r), 0, (i1 - i0) * P), ACT.Copy).then_inc(s_pT, 1)

                        exp(0, 0)
                        exp(0, 1)
                        for t in range(LT):
                            take_probs(t, 0)
                            take_probs(t, 1)
                            if t + 1 < LT:
                                exp(t + 1, 0)
                            take_probs(t, 2)
                            if t + 1 < LT:
                                exp(t + 1, 1)
                            if t:
                                outT(t - 1)
                        outT(LT - 1)

                @block.vector
                def _(dve):
                    dve.wait_ge(s_lin, 48)
                    for n in range(2):
                        nc.vector.tensor_tensor_reduce(out=lamt[:, n, :], in0=lam[:, 2 * n, :], in1=lam[:, 2 * n + 1, :],
                                                       scale=1.0, scalar=0.0, op0=ALU.mult, op1=ALU.add,
                                                       accum_out=lams[:, n:n + 1]).then_inc(s_lam, 1)
                    dve.wait_ge(s_lam, 3)
                    nc.vector.tensor_tensor(lams[:, 4:5], lams[:, 2:3], lams[:, 3:4], ALU.subtract).then_inc(s_lam, 1)
                    dve.wait_ge(s_lam, 4)
                    nc.vector.tensor_scalar(lams[:, 5:6], lams[:, 4:5], LAM_INIT, -1.0, ALU.add, ALU.mult).then_inc(s_lam, 1)
                    nc.vector.tensor_scalar(gsub[:, :], gsub[:, :], 1.0 - LAM_INIT, None, ALU.mult).then_inc(s_lam, 1)
                    dve.wait_ge(s_lam, 6)
                    with dve.Fori(0, GROUPS) as g:
                        for n in range(3):
                            kind, t0, w = chunks[NQK + n]
                            dve.wait_ge(s_mm, g * NM + NQK + n + 2)
                            nc.vector.tensor_copy(V[:, t0:t0 + w, :], bank((NQK + n) % 6, 0, w * P).rearrange("p (t n) -> p t n", n=P)).then_inc(s_v, 1)
                        for r in range(NROT):
                            i, cols = rot(r)
                            dst = (qT, kT)[i][:, cols]
                            dve.wait_ge(s_rop, g * NROT + r + 1)
                            nc.vector.tensor_tensor(dst, bank((2, 3, 4, 6)[r]), trig[:, 1, cols], ALU.mult).then_inc(s_sin, 1)
                            dve.wait_ge(s_sin, g * NROT + r + 1)
                            dve.wait_ge(s_cos, g * NROT + r + 1)
                            nc.vector.tensor_tensor(dst, dst, rq[:, i, cols], ALU.add).then_inc(s_rot, 1)

                        def mxcol(t, m):
                            return slice(2 * (t % 2) + m, 2 * (t % 2) + m + 1)

                        def maximum(t, m):
                            dve.wait_ge(s_S, g * 2 * LT + 2 * t + m + 1)
                            nc.vector.tensor_reduce(mx[:, mxcol(t, m)], S(m), AX.X, ALU.max, negate=True).then_inc(s_max, 1)

                        def combine(t):
                            dve.wait_ge(s_exp, g * 2 * LT + 2 * t + 2)
                            two = slice(2 * (t % 2), 2 * (t % 2) + 2)
                            nc.vector.reciprocal(rl[:, two], ls[:, two]).then_inc(s_cf, 1)
                            dve.wait_ge(s_cf, g * 2 * LT + 2 * t + 1)
                            nc.vector.scalar_tensor_tensor(out=cf[:, t % 2:t % 2 + 1], in0=ls[:, mxcol(t, 0)], scalar=rl[:, mxcol(t, 1)],
                                                           in1=lams[:, 5:6], op0=ALU.mult, op1=ALU.mult).then_inc(s_cf, 1)
                            dve.wait_ge(s_cf, g * 2 * LT + 2 * t + 2)
                            for dst, src in ((slice(SEQ, NTOK), slice(0, CTX)), (slice(0, SEQ), slice(CTX, NTOK))):
                                last = nc.vector.scalar_tensor_tensor(out=pb[:, t % 2, dst], in0=pb[:, 2, src], scalar=cf[:, t % 2:t % 2 + 1],
                                                                      in1=pb[:, t % 2, dst], op0=ALU.mult, op1=ALU.add)
                            last.then_inc(s_dif, 1)

                        def finish(t):
                            dve.wait_ge(s_o, g * LT + t + 1)
                            nc.vector.tensor_scalar(oraw[:, t % 2, :], O, rl[:, mxcol(t, 0)], None, ALU.mult).then_inc(s_on, 1)

                        def normalise(t):
                            base = g * 4 * LT + 4 * t
                            dve.wait_ge(s_on, base + 1)
                            nc.vector.tensor_tensor_reduce(out=osq[:, :], in0=oraw[:, t % 2, :], in1=oraw[:, t % 2, :], scale=1.0,
                                                           scalar=0.0, op0=ALU.mult, op1=ALU.add, accum_out=oss[:, 0:1]).then_inc(s_on, 1)
                            dve.wait_ge(s_on, base + 2)
                            nc.vector.tensor_scalar(oss[:, 1:2], oss[:, 0:1], 1.0 / P, EPS, ALU.mult, ALU.add).then_inc(s_on, 1)
                            dve.wait_ge(s_on, base + 4)
                            if t >= 2:
                                dve.wait_ge(s_oTp, g * LT + t - 1)
                            nc.vector.tensor_scalar(osb[:, t % 2, :], oraw[:, t % 2, :], oss[:, 2:3], None, ALU.mult).then_inc(s_osb, 1)

                        maximum(0, 0)
                        maximum(0, 1)
                        combine(0)
                        for t in range(LT):
                            if t + 1 < LT:
                                maximum(t + 1, 0)
                                maximum(t + 1, 1)
                            finish(t)
                            if t + 1 < LT:
                                combine(t + 1)
                            normalise(t)

        def project_out(l, hT, oT, wo_in):
            T = NT if l == 0 else LT
            with ExitStack() as c:
                tmp = sb(c, "gated", [P, 4, HALF])
                s_y, s_g, s_r = (sem(c, n) for n in ("y_ready", "y_gated", "residual_added"))
                block = c.enter_context(nc.Block())

                @block.tensor
                def _(pe):
                    pe.wait_ge(wo_in, 16 * (4 + (2 if l == 0 else 1)))
                    for n in range(2 * T):
                        t, h = n // 2, n % 2
                        if n >= 4:
                            pe.wait_ge(s_g, n - 3)
                        for k in range(KD):
                            m = nc.tensor.matmul(bank(n % 4), oT[:, k * NTOK + t * P:k * NTOK + (t + 1) * P],
                                                 hT[:, k, h * HALF:(h + 1) * HALF], start=k == 0, stop=k == KD - 1)
                        m.then_inc(s_y, 1)

                @block.vector
                def _(dve):
                    dve.wait_ge(wo_in, 16 * (4 + (2 if l == 0 else 1)))
                    for n in range(2 * T):
                        t, h = n // 2, n % 2
                        dve.wait_ge(s_y, n + 1)
                        if n >= 4:
                            dve.wait_ge(s_r, n - 3)
                        nc.vector.tensor_tensor(tmp[:, n % 4, :], bank(n % 4), rows[:, 2 if t >= LT else 3, h * HALF:(h + 1) * HALF],
                                                ALU.mult).then_inc(s_g, 1)

                @block.gpsimd
                def _(pool):
                    for n in range(2 * T):
                        t, h = n // 2, n % 2
                        pool.wait_ge(s_g, n + 1)
                        xs = x[:, t, h * HALF:(h + 1) * HALF]
                        nc.gpsimd.tensor_tensor(xs, xs, tmp[:, n % 4, :], ALU.add).then_inc(s_r, 1)

        def routing(l):
            T = TILES[l]
            C = CAP[l]
            W = T * NE
            with ExitStack() as c:
                r = lambda name, n, dt=F32: sb(c, name, [P, n], dt)
                sc, sel, msel, w16, oh1, oh2, ohs, cum, pos, t16 = (r(n, W) for n in (
                    "rt_scores", "rt_sel", "rt_masked", "rt_w16", "rt_first", "rt_second", "rt_chosen", "rt_before", "rt_pos", "rt_t16"))
                hi, lo, g4a, g4b, gw = (r(n, T * NG * 2) for n in ("rt_hi", "rt_lo", "rt_g4a", "rt_g4b", "rt_gw"))
                t1, gt, s2 = r("rt_t1", T), r("rt_gt", T * 2), r("rt_s2", T * 2)
                rb = r("rt_bias", NE)
                tot, nch, cend, cbuf, base = (r(n, NE) for n in ("rt_total", "rt_chunks", "rt_end", "rt_endb", "rt_base"))
                cmpb = r("rt_compare", NE * 16)
                tab = r("rt_table", 64)
                cmpt = r("rt_compare_items", 64 * NE)
                slotf = r("rt_slotf", T * 2)
                tok = sb(c, "rt_tok", [P, NT, 16], I32)
                s_in, s_sig, s_ch, s_cnt, s_pos, s_tok, s_tab, s_slot = (sem(c, n) for n in (
                    "rt_in", "rt_sigmoid", "rt_chain", "rt_counted", "rt_ranked", "rt_tok_in", "rt_table_done", "rt_scattered"))
                block = c.enter_context(nc.Block())
                bc = lambda ap, shape: ap.to_broadcast(shape)
                CH_OH, CH_SLOT = [0], [0]

                @block.sync
                def _(sp):
                    sp.dma_start(rb[:, :], a["router_b"].partition_broadcast(P)).then_inc(s_in, 16)
                    sp.dma_start(tok[:, :, :], a["tokens"]).then_inc(s_tok, 16)

                @block.scalar
                def _(act):
                    nc.scalar.activation(sc[:, :], bank(7, 0, W), ACT.Sigmoid).then_inc(s_sig, 1)

                @block.vector
                def _(dve):
                    ch = Steps(dve, s_ch)
                    v = nc.vector
                    TE = lambda z: z[:, 0:W].rearrange("p (t e) -> p t e", e=NE)
                    TGE = lambda z: z[:, 0:W].rearrange("p (t g e) -> p t g e", g=NG, e=EPG)
                    TG = lambda z: z[:, 0:T * NG].rearrange("p (t g) -> p t g", g=NG)
                    TG2 = lambda z: z[:, 0:T * NG * 2].rearrange("p (t g b) -> p t g b", g=NG, b=2)
                    pair = lambda z, i: z[:, 0:W].rearrange("p (t g b i) -> p t g b i", g=NG, b=2, i=2)[:, :, :, :, i]
                    dve.wait_ge(s_in, 16)
                    dve.wait_ge(s_sig, 1)
                    ch.then(v.tensor_tensor(TE(sel), TE(sc), bc(rb[:, :].unsqueeze(1), [P, T, NE]), ALU.add))
                    flat_pairs = sel[:, :].rearrange("p (n i) -> p n i", i=2)
                    v.tensor_tensor(lo[:, 0:W // 2], flat_pairs[:, :, 0], flat_pairs[:, :, 1], ALU.min)
                    ch.then(v.tensor_tensor(hi[:, 0:W // 2], flat_pairs[:, :, 0], flat_pairs[:, :, 1], ALU.max))
                    h2 = hi[:, 0:W // 2].rearrange("p (n i) -> p n i", i=2)
                    l2 = lo[:, 0:W // 2].rearrange("p (n i) -> p n i", i=2)
                    N4 = T * NG
                    v.tensor_tensor(g4a[:, 0:N4], h2[:, :, 0], h2[:, :, 1], ALU.max)
                    v.tensor_tensor(g4b[:, 0:N4], h2[:, :, 0], h2[:, :, 1], ALU.min)
                    ch.then(v.tensor_tensor(gw[:, 0:N4], l2[:, :, 0], l2[:, :, 1], ALU.max))
                    ch.then(v.tensor_tensor(g4b[:, 0:N4], g4b[:, 0:N4], gw[:, 0:N4], ALU.max))
                    ch.then(v.tensor_tensor(g4a[:, 0:N4], g4a[:, 0:N4], g4b[:, 0:N4], ALU.add))

                    def first_of_max(dst, src, n, prio):
                        vv = lambda z: z[:, 0:T * n].rearrange("p (t e) -> p t e", e=n)
                        ch.then(v.tensor_reduce(t1[:, :], vv(src), AX.X, ALU.max))
                        ch.then(v.tensor_tensor(vv(dst), vv(src), bc(t1[:, :].unsqueeze(2), [P, T, n]), ALU.is_equal))
                        ch.then(v.tensor_tensor(vv(dst), vv(dst), bc(prio.unsqueeze(1), [P, T, n]), ALU.mult))
                        ch.then(v.tensor_reduce(t1[:, :], vv(dst), AX.X, ALU.max))
                        ch.then(v.tensor_tensor(vv(dst), vv(dst), bc(t1[:, :].unsqueeze(2), [P, T, n]), ALU.is_equal))

                    first_of_max(gw, g4a, NG, con[:, C_P4:C_P16])
                    ch.then(v.tensor_scalar(g4b[:, 0:N4], gw[:, 0:N4], -1.0, -NEG, ALU.add, ALU.mult))
                    gsel = bc(gw[:, 0:N4].rearrange("p (n i) -> p n i", i=1), [P, N4, EPG])
                    goff = bc(g4b[:, 0:N4].rearrange("p (n i) -> p n i", i=1), [P, N4, EPG])
                    n4 = lambda z: z[:, :].rearrange("p (n e) -> p n e", e=EPG)
                    ch.then(v.tensor_tensor(n4(msel), n4(sel), gsel, ALU.mult))
                    ch.then(v.tensor_tensor(n4(msel), n4(msel), goff, ALU.add))
                    first_of_max(oh1, msel, NE, con[:, C_P16:C_THR])
                    ch.then(v.scalar_tensor_tensor(out=msel[:, :], in0=oh1[:, :], scalar=NEG, in1=msel[:, :], op0=ALU.mult, op1=ALU.add))
                    first_of_max(oh2, msel, NE, con[:, C_P16:C_THR])
                    ch.then(v.tensor_tensor(ohs[:, :], oh1[:, :], oh2[:, :], ALU.add))
                    ch.then(v.memset(cum[:, 0:NE], 0.0))
                    for t in range(1, T):
                        ch.then(v.tensor_tensor(cum[:, t * NE:(t + 1) * NE], cum[:, (t - 1) * NE:t * NE], ohs[:, (t - 1) * NE:t * NE], ALU.add))
                    ch.then(v.tensor_tensor(tot[:, :], cum[:, (T - 1) * NE:], ohs[:, (T - 1) * NE:], ALU.add))
                    CH_OH[0] = ch.n
                    for i, oh in enumerate((oh1, oh2)):
                        ch.then(v.tensor_tensor(t16[:, :], sc[:, :], oh[:, :], ALU.mult))
                        ch.then(v.tensor_reduce(gt[:, i * T:(i + 1) * T], TE(t16), AX.X, ALU.add))
                    ch.then(v.tensor_tensor(t1[:, :], gt[:, 0:T], gt[:, T:2 * T], ALU.add))
                    ch.then(v.reciprocal(t1[:, :], t1[:, :]))
                    for i in range(2):
                        ch.then(v.tensor_tensor(gates[:, 0:T, i], gt[:, i * T:(i + 1) * T], t1[:, :], ALU.mult))
                    dve.wait_ge(s_cnt, 1)
                    ch.then(v.tensor_scalar(tot[:, :], bank(6, 256, 256 + NE), 1.0 / C, None, ALU.mult))
                    c3 = cmpb[:, :].rearrange("p (e j) -> p e j", j=16)
                    ch.then(v.tensor_tensor(c3, bc(tot[:, :].unsqueeze(2), [P, NE, 16]), bc(con[:, C_THR:C_IOTA].unsqueeze(1), [P, NE, 16]), ALU.is_gt))
                    ch.then(v.tensor_reduce(nch[:, :], c3, AX.X, ALU.add))
                    ch.then(v.tensor_scalar(cend[:, :], nch[:, :], 1.0, None, ALU.add))
                    src, dst = cend, cbuf
                    ch.then(v.tensor_copy(nch[:, :], cend[:, :]))
                    for k in (1, 2, 4, 8):
                        ch.then(v.tensor_copy(dst[:, 0:k], src[:, 0:k]))
                        ch.then(v.tensor_tensor(dst[:, k:], src[:, k:], src[:, 0:NE - k], ALU.add))
                        src, dst = dst, src
                    ch.then(v.tensor_tensor(base[:, :], src[:, :], nch[:, :], ALU.subtract))
                    ch.then(v.tensor_scalar(base[:, :], base[:, :], float(C), None, ALU.mult))
                    ch.then(v.tensor_copy(nitem[:, :], src[:, NE - 1:NE]))
                    i3 = cmpt[:, :].rearrange("p (i e) -> p i e", e=NE)
                    ch.then(v.tensor_tensor(i3, bc(con[:, C_IOTA:C_HALF].unsqueeze(2), [P, 64, NE]), bc(src[:, :].unsqueeze(1), [P, 64, NE]), ALU.is_ge))
                    ch.then(v.tensor_reduce(tab[:, :], i3, AX.X, ALU.add))
                    ch.then(v.tensor_scalar(table[:, :], tab[:, :], float(NE - 1), None, ALU.min))
                    dve.wait_ge(s_pos, 1)
                    ch.then(v.tensor_tensor(TE(pos), bank(6, 0, W).rearrange("p (t e) -> p t e", e=NE), bc(base[:, :].unsqueeze(1), [P, T, NE]), ALU.add))
                    for i, oh in enumerate((oh1, oh2)):
                        ch.then(v.tensor_tensor(t16[:, :], pos[:, :], oh[:, :], ALU.mult))
                        ch.then(v.tensor_reduce(slotf[:, i * T:(i + 1) * T], TE(t16), AX.X, ALU.add))
                        ch.then(v.tensor_copy(slots[:, 0:T, i], slotf[:, i * T:(i + 1) * T]))
                    CH_SLOT[0] = ch.n

                @block.tensor
                def _(pe):
                    pe.wait_ge(s_ch, CH_OH[0])
                    nc.tensor.matmul(bank(6, 0, W), con[:, C_TRI:C_TRI + P], ohs[:, :], start=True, stop=False)
                    nc.tensor.matmul(bank(6, 0, W), con[:, C_ONE:C_ONE + P], cum[:, :], start=False, stop=True).then_inc(s_pos, 1)
                    nc.tensor.matmul(bank(6, 256, 256 + NE), con[:, C_ONE:C_ONE + P], tot[:, :], start=True, stop=True).then_inc(s_cnt, 1)

                @block.gpsimd
                def _(pool):
                    pool.wait_ge(s_tok, 16)
                    pool.wait_ge(s_ch, CH_SLOT[0])
                    for t in range(T):
                        for i in range(2):
                            nc.gpsimd.indirect_dma_start(out=idx_dram[l], out_offset=bass.IndirectOffsetOnAxis(slots[:, t, i:i + 1], 0),
                                                         in_=tok[:, t, :], in_offset=None).then_inc(s_slot, 16)
                    pool.wait_ge(s_slot, 16 * 2 * T)

        def experts(l):
            C = CAP[l]
            R = C - P
            FB = D // P
            with ExitStack() as c:
                ring = sb(c, "expert_ring", [P, 6, KD, HALF])
                idx = sb(c, "slot_idx", [P, 2, 16], I32)
                xg = sb(c, "gathered", [P, 2, D])
                xT = sb(c, "item_xT", [P, KD, C])
                aT = sb(c, "item_aT", [P, FB, C])
                sg = sb(c, "item_silu", [P, 2, C])
                yT = sb(c, "item_yT", [P, 2, C])
                yr = sb(c, "item_y", [P, 2, D])
                p_in = [sem(c, f"piece_in{n}") for n in range(6)]
                s_ix, s_xg, s_xt, s_xT, s_gu, s_sg, s_a, s_y, s_yT, s_yt, s_yr, s_st, s_go = (sem(c, n) for n in (
                    "idx_in", "x_gathered", "x_transposed", "xT_ready", "gate_up", "silu_done", "hidden_ready",
                    "down_ready", "yT_ready", "y_transposed", "y_rows", "y_stored", "waited"))
                block = c.enter_context(nc.Block())
                rows_of = lambda w: w.rearrange("l e d f -> (l e d) f")
                wg, wu, wd = (rows_of(a[n]) for n in ("expert_w_gate", "expert_w_up", "expert_w_down"))
                gub = lambda b, w: bank(b % 2, w * 256, w * 256 + C)
                yb = lambda j: bank(2 + j % 2, 0, C)
                xtb = lambda r: bank(4 + r % 2)
                count = lambda eng: eng.value_load(nitem[0:1, 0:1], min_val=NE, max_val=ITEMS[l])

                @block.sync
                def _(sp):
                    n = count(sp)
                    with sp.Fori(0, n) as i:
                        e = sp.value_load(table[0:1, bass.ds(i, 1)], min_val=0, max_val=NE - 1)
                        part = lambda w: w[bass.ds((e + l * NE) * D, D), :].rearrange("(k p) f -> p k f", p=P)
                        for q in range(6):
                            if q < 4:
                                sp.wait_ge(s_gu, i * 8 + 2 * q + 2)
                            else:
                                sp.wait_ge(s_y, i * 8 + 4 * (q - 4) + 4)
                            if q < 4:
                                sp.dma_start(ring[:, q, :, 0:256], part(wg)[:, :, q * 256:(q + 1) * 256]).then_inc(p_in[q], 16)
                                sp.dma_start(ring[:, q, :, 256:512], part(wu)[:, :, q * 256:(q + 1) * 256]).then_inc(p_in[q], 16)
                            else:
                                sp.dma_start(ring[:, q], part(wd)[:, :, (q - 4) * HALF:(q - 3) * HALF]).then_inc(p_in[q], 16)

                def gather(pool, j):
                    pool.dma_start(idx[:, 0, :], idx_dram[l][bass.ds(j * C, P), :]).then_inc(s_ix, 16)
                    pool.dma_start(idx[0:R, 1, :], idx_dram[l][bass.ds(j * C + P, R), :]).then_inc(s_ix, 16)
                    pool.wait_ge(s_ix, (j + 1) * 32)
                    pool.wait_ge(s_xt, j * 4 + 4)
                    pool.sem_inc(s_go, 1)
                    nc.gpsimd.indirect_dma_start(out=xg[:, 0, :], out_offset=None, in_=h_dram,
                                                 in_offset=bass.IndirectOffsetOnAxis(idx[:, 0, 0:1], 0)).then_inc(s_xg, 16)
                    nc.gpsimd.indirect_dma_start(out=xg[0:R, 1, :], out_offset=None, in_=h_dram,
                                                 in_offset=bass.IndirectOffsetOnAxis(idx[0:R, 1, 0:1], 0)).then_inc(s_xg, 16)
                    pool.wait_ge(s_xg, (j + 1) * 32)

                @block.gpsimd
                def _(pool):
                    n = count(pool)
                    pool.sem_inc(s_xt, 4)
                    gather(pool, 0)
                    with pool.Fori(0, n) as i:
                        gather(pool, i + 1)

                @block.tensor
                def _(pe):
                    n = count(pe)
                    pe.sem_inc(s_gu, 8)
                    pe.sem_inc(s_y, 8)

                    def transposes(j):
                        pe.wait_ge(s_xg, (j + 1) * 32)
                        for r in range(4):
                            if r >= 2:
                                pe.wait_ge(s_xT, j * 4 + r - 1)
                            for k in (2 * r, 2 * r + 1):
                                o = (k % 2) * 256
                                nc.tensor.transpose(xtb(r)[:, o:o + P], xg[:, 0, k * P:(k + 1) * P], ident)
                                m = nc.tensor.transpose(xtb(r)[:, o + P:o + C], xg[0:R, 1, k * P:(k + 1) * P], ident[0:R, 0:R])
                            m.then_inc(s_xt, 1)

                    transposes(0)
                    with pe.Fori(0, n) as i:
                        pe.wait_ge(s_xT, i * 4 + 4)
                        for b in range(FB):
                            if b % 2 == 0:
                                pe.wait_ge(p_in[b // 2], i * 32 + 32)
                            if b >= 2:
                                pe.wait_ge(s_a, i * 8 + b - 1)
                            for w in range(2):
                                for k in range(KD):
                                    m = nc.tensor.matmul(gub(b, w), ring[:, b // 2, k, w * 256 + (b % 2) * P:w * 256 + (b % 2 + 1) * P],
                                                         xT[:, k, :], start=k == 0, stop=k == KD - 1)
                            m.then_inc(s_gu, 1)
                        transposes(i + 1)

                        def back(j):
                            pe.wait_ge(s_yT, i * 8 + j + 1)
                            if j % 4 == 0:
                                pe.wait_ge(s_yr, i * 2 + j // 4 + 1)
                            o = (j % 4) * P
                            nc.tensor.transpose(bank(6, o, o + P), yT[:, j % 2, 0:P], ident)
                            m = nc.tensor.transpose(bank(7)[0:R, o:o + P], yT[:, j % 2, P:C], ident)
                            if j % 4 == 3:
                                m.then_inc(s_yt, 1)

                        pe.wait_ge(s_a, i * 8 + 8)
                        for j in range(KD):
                            if j % 4 == 0:
                                pe.wait_ge(p_in[4 + j // 4], i * 16 + 16)
                            for f in range(FB):
                                m = nc.tensor.matmul(yb(j), ring[:, 4 + j // 4, f, (j % 4) * P:(j % 4 + 1) * P], aT[:, f, :],
                                                     start=f == 0, stop=f == FB - 1)
                            m.then_inc(s_y, 1)
                            if j:
                                back(j - 1)
                        back(KD - 1)

                @block.scalar
                def _(act):
                    n = count(act)
                    act.sem_inc(s_st, 1)
                    with act.Fori(0, n) as i:
                        for b in range(FB):
                            act.wait_ge(s_gu, i * 8 + b + 9)
                            nc.scalar.activation(sg[:, b % 2, :], gub(b, 0), ACT.Silu).then_inc(s_sg, 1)
                        for j in range(KD):
                            act.wait_ge(s_y, i * 8 + j + 9)
                            nc.scalar.activation(yT[:, j % 2, :], yb(j), ACT.Copy).then_inc(s_yT, 1)
                        act.wait_ge(s_yr, i * 2 + 3)
                        act.dma_start(ys[bass.ds(i * C, P), :], yr[:, 0, :]).then_inc(s_st, 16)
                        act.dma_start(ys[bass.ds(i * C + P, R), :], yr[0:R, 1, :]).then_inc(s_st, 16)
                    act.wait_ge(s_st, n * 32 + 1)
                    act.sem_inc(s_go, 1)

                @block.vector
                def _(dve):
                    n = count(dve)
                    dve.sem_inc(s_yr, 1)

                    def take_x(j):
                        for r in range(4):
                            dve.wait_ge(s_xt, j * 4 + r + 5)
                            nc.vector.tensor_copy(xT[:, 2 * r:2 * r + 2, :],
                                                  xtb(r).rearrange("p (k c) -> p k c", c=256)[:, :, 0:C]).then_inc(s_xT, 1)

                    take_x(0)
                    with dve.Fori(0, n) as i:
                        for b in range(FB):
                            dve.wait_ge(s_sg, i * 8 + b + 1)
                            nc.vector.tensor_tensor(aT[:, b, :], sg[:, b % 2, :], gub(b, 1), ALU.mult).then_inc(s_a, 1)
                        take_x(i + 1)
                        for h in range(2):
                            dve.wait_ge(s_yt, i * 2 + h + 1)
                            if h == 0:
                                dve.wait_ge(s_st, i * 32 + 1)
                            nc.vector.tensor_copy(yr[0:R, 1, h * HALF:(h + 1) * HALF], bank(7)[0:R, :])
                            nc.vector.tensor_copy(yr[:, 0, h * HALF:(h + 1) * HALF], bank(6)).then_inc(s_yr, 1)

        def combine_experts(l):
            T = TILES[l]
            with ExitStack() as c:
                y = sb(c, "y_pair", [P, 3, 2, D])
                s_r, s_m, s_c, s_g, s_x = (sem(c, n) for n in ("gate_rows_in", "y_first", "y_sum", "y_gate", "x_added"))
                s_in = [sem(c, f"y_in{n}") for n in range(3)]
                block = c.enter_context(nc.Block())

                @block.sync
                def _(sp):
                    for v in range(2 if T > LT else 1):
                        sp.dma_start(rows[:, v, :], mods[l, v, 5 * D:6 * D].partition_broadcast(P)).then_inc(s_r, 16)

                @block.gpsimd
                def _(pool):
                    for t in range(T):
                        if t >= 3:
                            pool.wait_ge(s_x, t - 2)
                        for i in range(2):
                            nc.gpsimd.indirect_dma_start(out=y[:, t % 3, i, :], out_offset=None, in_=ys,
                                                         in_offset=bass.IndirectOffsetOnAxis(slots[:, t, i:i + 1], 0)).then_inc(s_in[t % 3], 16)

                @block.scalar
                def _(act):
                    for t in range(T):
                        act.wait_ge(s_in[t % 3], 32 * (t // 3 + 1))
                        nc.scalar.activation(y[:, t % 3, 0, :], y[:, t % 3, 0, :], ACT.Copy, scale=gates[:, t, 0:1]).then_inc(s_m, 1)

                @block.vector
                def _(dve):
                    dve.wait_ge(s_r, 32 if T > LT else 16)
                    for t in range(T):
                        y0, y1 = y[:, t % 3, 0, :], y[:, t % 3, 1, :]
                        dve.wait_ge(s_m, t + 1)
                        nc.vector.scalar_tensor_tensor(out=y0, in0=y1, scalar=gates[:, t, 1:2], in1=y0, op0=ALU.mult, op1=ALU.add).then_inc(s_c, 1)
                        dve.wait_ge(s_c, t + 1)
                        nc.vector.tensor_tensor(y0, y0, rows[:, 1 if t >= LT else 0, :], ALU.mult).then_inc(s_g, 1)
                        dve.wait_ge(s_g, t + 1)
                        nc.vector.tensor_tensor(x[:, t, :], x[:, t, :], y0, ALU.add).then_inc(s_x, 1)

        def final():
            with ExitStack() as c:
                junk = sb(c, "fin_junk", [P, D])
                ob = sb(c, "fin_out", [P, 3, D])
                s_r, s_ss, s_rs, s_o = (sem(c, n) for n in ("fin_rows", "fin_ss", "fin_rstd", "fin_ready"))
                s_st = [sem(c, f"fin_stored{n}") for n in range(3)]
                block = c.enter_context(nc.Block())

                @block.scalar
                def _(act):
                    for t in range(LT):
                        if t:
                            act.wait_ge(s_ss, t)
                        nc.scalar.activation(junk[:, :], x[:, t, :], ACT.Square, accum_out=ss[:, t:t + 1]).then_inc(s_ss, 1)

                @block.vector
                def _(dve):
                    dve.wait_ge(s_ss, LT)
                    nc.vector.tensor_scalar(std[:, 0:LT], ss[:, 0:LT], 1.0 / D, EPS, ALU.mult, ALU.add).then_inc(s_rs, 1)
                    dve.wait_ge(s_rs, 2)
                    dve.wait_ge(s_r, 16)
                    for t in range(LT):
                        if t >= 3:
                            dve.wait_ge(s_st[t % 3], 16 * (t // 3))
                        nc.vector.scalar_tensor_tensor(out=ob[:, t % 3, :], in0=x[:, t, :], scalar=rstd[:, t:t + 1], in1=rows[:, 0, :],
                                                       op0=ALU.mult, op1=ALU.mult).then_inc(s_o, 1)

                @block.gpsimd
                def _(pool):
                    pool.wait_ge(s_rs, 1)
                    nc.gpsimd.tensor_tensor(rstd[:, 0:LT], std[:, 0:LT], con[:, C_HALF:C_HALF + LT], ALU.pow).then_inc(s_rs, 1)

                @block.sync
                def _(sp):
                    sp.dma_start(rows[:, 0, :], a["final_norm"].partition_broadcast(P)).then_inc(s_r, 16)
                    for t in range(LT):
                        sp.wait_ge(s_o, t + 1)
                        sp.dma_start(out[0, t * P:(t + 1) * P, :], ob[:, t % 3, :]).then_inc(s_st[t % 3], 16)
                    for n in range(3):
                        sp.wait_ge(s_st[n], 16 * len(range(n, LT, 3)))

        modulation()
        for l in range(2):
            with ExitStack() as c:
                hT = sb(c, "hT", [P, KD, NTOK])
                oT = sb(c, "oT", [P, KD * NTOK])
                wo_in = sem(c, "wo_in")
                normed(l, False, hT)
                (neighbourhood if l == 0 else differential)(hT, oT, wo_in)
                project_out(l, hT, oT, wo_in)
            with ExitStack() as c:
                hT = sb(c, "hT_ffn", [P, KD, NTOK])
                rw = sb(c, "router_w", [P, KD, NE])
                normed(l, True, hT, rw)
            routing(l)
            experts(l)
            combine_experts(l)
            if l == 0:
                nc.all_engine_barrier()
                nc.clear_and_free_semaphores(list(stage_sems))
                nc.all_engine_barrier()
        final()


_INS = ["x", "c", "ctx", "c_ctx", "mod_w", "mod_b", "norm_mix", "norm_ffn", "w_qkv", "w_o", "diff_lambda", "diff_subln",
        "router_w", "router_b", "expert_w_gate", "expert_w_up", "expert_w_down", "final_norm"]


def kernel(**inputs):
    import numpy as _np
    import concourse.bacc as _bacc
    from concourse import mybir as _mybir
    from concourse.bass_utils import run_bass_kernel_spmd as _run

    nc = _bacc.Bacc("TRN2", target_bir_lowering=False, num_devices=1)
    host = {name: _np.ascontiguousarray(inputs[name]) for name in _INS}
    host["consts"], host["trig"], host["tokens"] = shape_constants()
    rpb = _np.ascontiguousarray(inputs["na_rpb"])[0]
    pad = _np.zeros((16, 15, P), _np.float32)
    pad[:, :, GRID_W - WIN_COLS:GRID_W + WIN_COLS - 1] = rpb
    host["rpb_pad"] = pad
    arrays, args = {}, {}
    for name, v in host.items():
        arrays[f"in_{name}"] = v
        args[name] = nc.dram_tensor(f"in_{name}", v.shape, _mybir.dt.from_np(v.dtype), kind="ExternalInput").ap()
    args["out"] = nc.dram_tensor("out_0", (1, SEQ, D), _mybir.dt.float32, kind="ExternalOutput").ap()
    build(nc, args)
    r = _run(nc, [arrays], core_ids=[0])
    return r.results[0]["out_0"]
```

```python
import math
from contextlib import ExitStack

import concourse.bass as bass
import numpy as np
from concourse import mybir

F32 = mybir.dt.float32
F32R = mybir.dt.float32r
I32 = mybir.dt.int32
ACT = mybir.ActivationFunctionType
ALU = mybir.AluOpType
AX = mybir.AxisListType

P = 128
D = 1024
KD = D // P
SEQ, CTX = 1024, 256
LT, CT = SEQ // P, CTX // P
NT = LT + CT
NTOK = SEQ + CTX
GRID_W = 64
HALF = 512
NMOD = 6
NE, NG, EPG = 16, 4, 4
EPS = 1e-6
NEG = -1.0e30
HD = 64
SCALE = HD ** -0.5
GROUPS = D // P
WIN_ROWS, WIN_COLS = 8, 16
TABR = 14
INTR = 10
CAP = (160, 144)
TILES = (NT, LT)
ITEMS = tuple(NE + (2 * TILES[l] * P) // CAP[l] for l in range(2))
LAM_INIT = 0.8 - 0.6 * math.exp(-0.3 * (2 - 1))

C_ID, C_TRI, C_ONE, C_PERM = 0, 128, 256, 384
C_EDGE = 512
C_INT = C_EDGE + GRID_W
C_P4 = C_INT + INTR * GRID_W
C_P16 = C_P4 + NG
C_THR = C_P16 + NE
C_IOTA = C_THR + 16
C_HALF = C_IOTA + 64
C_ALL = C_HALF + 16


def shape_constants():
    c = np.zeros((P, C_ALL), np.float32)
    p = np.arange(P)
    c[:, C_ID:C_ID + P] = np.eye(P)
    c[:, C_TRI:C_TRI + P] = p[:, None] < p[None, :]
    c[:, C_ONE:C_ONE + P] = 1
    c[:, C_PERM:C_PERM + P] = p[:, None] == (p[None, :] ^ 32)
    q, rp = p % GRID_W, p // GRID_W
    start = np.clip(q - WIN_COLS // 2, 0, GRID_W - WIN_COLS)
    k = np.arange(GRID_W)
    inside = (k[None] >= start[:, None]) & (k[None] < start[:, None] + WIN_COLS)
    c[:, C_EDGE:C_EDGE + GRID_W] = np.where(inside, 0, NEG)
    j = np.arange(INTR)
    rows = (j[None] >= rp[:, None]) & (j[None] < rp[:, None] + WIN_ROWS)
    c[:, C_INT:C_P4] = np.where(rows[:, :, None] & inside[:, None, :], 0, NEG).reshape(P, -1)
    c[:, C_P4:C_P16] = NG - np.arange(NG)
    c[:, C_P16:C_THR] = NE - np.arange(NE)
    c[:, C_THR:C_IOTA] = 1 + np.arange(16)
    c[:, C_IOTA:C_HALF] = np.arange(64)
    c[:, C_HALF:] = -0.5
    t = np.arange(SEQ)
    freq = np.float32(10000.0) ** (-np.arange(16, dtype=np.float32) / 16)
    ang = np.concatenate([(t // GRID_W).astype(np.float32)[:, None] * freq,
                          (t % GRID_W).astype(np.float32)[:, None] * freq], axis=-1)
    cos, sin = np.cos(ang).T, np.sin(ang).T
    trig = np.concatenate([np.tile(cos, (4, 1)), np.concatenate([-sin, sin, -sin, sin])], axis=1)
    tok = np.broadcast_to((np.arange(NT)[None, :] * P + p[:, None])[:, :, None], (P, NT, 16))
    return c, np.ascontiguousarray(trig, np.float32), np.ascontiguousarray(tok, np.int32)


class Steps:

    def __init__(self, eng, sem, base=0):
        self.eng, self.sem, self.base, self.n = eng, sem, base, 0

    def then(self, ins):
        ins.then_inc(self.sem, 1)
        self.n += 1
        self.eng.wait_ge(self.sem, self.base + self.n)


def window(t):
    if t >= LT:
        return 0, 0
    return (t - 2, 5) if 2 <= t < 6 else (0, 4) if t < 2 else (4, 4)


def build(nc, a):
    out = a["out"]
    dram = lambda name, shape, dt=F32: nc.dram_tensor(name, shape, dt, kind="Internal").ap()
    mods = dram("mods", [2, 2, NMOD * D])
    toep = dram("toep", [16, GRID_W, 15, GRID_W])
    h_dram = dram("h_rows", [NTOK, D])
    idx_dram = [dram(f"slot_token{l}", [(ITEMS[l] + 1) * CAP[l], 16], I32) for l in range(2)]
    ys = dram("slot_out", [max(ITEMS[l] * CAP[l] for l in range(2)), D])

    top = ExitStack()

    seen = {}

    def unique(name):
        seen[name] = seen.get(name, 0) + 1
        return name if seen[name] == 1 else f"{name}_{seen[name]}"

    def sb(c, name, shape, dt=F32):
        return c.enter_context(nc.sbuf_tensor(unique(name), shape, dt))

    stage_sems = []
    software = {"idx_cleared", "slots_cleared", "rt_scattered", "idx_in", "x_gathered", "y_in0", "y_in1", "y_in2"}

    def sem(c, name):
        handle = nc.alloc_semaphore(name=unique(name))
        if name not in software:
            stage_sems.append(handle)
        return handle

    with top:
        con = sb(top, "con", [P, C_ALL])
        rows = sb(top, "rows", [P, 4, D])
        ss = sb(top, "ss", [P, NT])
        std = sb(top, "std", [P, NT])
        rstd = sb(top, "rstd", [P, NT])
        slots = sb(top, "slots", [P, NT, 2], I32)
        gates = sb(top, "gates", [P, NT, 2])
        table = sb(top, "table", [P, 64], I32)
        nitem = sb(top, "nitem", [P, 1], I32)
        ps = top.enter_context(nc.psum_tensor("ps", [P, 8 * HALF], F32))
        bank = lambda n, c0=0, c1=HALF: ps[:, n * HALF + c0:n * HALF + c1]
        ident = con[:, C_ID:C_ID + P]

        def modulation():
            with ExitStack() as c:
                RING, STEP = 3, 6
                cc = sb(c, "cc", [P, 2, KD])
                cact = sb(c, "cact", [P, 2, KD])
                c_hi = sb(c, "c_high", [P, 2, KD], F32R)
                c_lo = sb(c, "c_low", [P, 2, KD], F32R)
                modr = sb(c, "modr", [2, 2, NMOD * D])
                gn = sb(c, "gn", [2, 2, 2, D])
                W = sb(c, "mod_ring", [P, RING, KD, HALF])
                W_hi = sb(c, "mod_high", [P, 2, KD, HALF], F32R)
                W_lo = sb(c, "mod_low", [P, 2, KD, HALF], F32R)
                zero = sb(c, "zero", [P, 1024], I32)
                NP = NMOD * D // HALF
                s_c, s_b, s_con = (sem(c, n) for n in ("c_in", "bias_in", "con_in"))
                w_in = [sem(c, f"modw_in{n}") for n in range(RING)]
                s_act, s_mm, s_add, s_rows, s_out, s_hi, s_lo = (sem(c, n) for n in (
                    "silu_done", "mod_mm", "mod_add", "mod_rows", "mod_out", "mod_w_high", "mod_w_low"))
                s_zero, s_idx = sem(c, "zero_set"), sem(c, "idx_cleared")
                block = c.enter_context(nc.Block())

                @block.sync
                def _(sp):
                    sp.dma_start(cc[:, 0, :], a["c"].rearrange("b (p k) -> p (b k)", k=KD)).then_inc(s_c, 16)
                    sp.dma_start(cc[:, 1, :], a["c_ctx"].rearrange("(p k) -> p k", k=KD)).then_inc(s_c, 16)
                    for l in range(2):
                        src = a["mod_w"][l].rearrange("(p k) n -> p k n", k=KD)
                        with sp.Fori(0, NP // STEP) as it:
                            for i in range(STEP):
                                sp.wait_ge(s_lo, it * STEP + l * NP + i + 1)
                                sp.dma_start(W[:, i % RING], src[:, :, bass.ds((it * STEP + i) * HALF, HALF)]).then_inc(w_in[i % RING], 16)
                    for l in range(2):
                        sp.wait_ge(s_rows, 2 * l + 2)
                        sp.dma_start(mods[l], modr[:, l, :]).then_inc(s_out, 16)
                    sp.wait_ge(s_out, 32)

                @block.scalar
                def _(act):
                    act.wait_ge(s_c, 32)
                    nc.scalar.activation(cact[:, :, :], cc[:, :, :], ACT.Silu).then_inc(s_act, 1)
                    act.wait_ge(s_act, 1)
                    nc.scalar.activation(c_hi[:, :, :], cact[:, :, :], ACT.Copy).then_inc(s_act, 1)
                    act.dma_start(con[:, :], a["consts"]).then_inc(s_con, 16)
                    for l in range(2):
                        act.dma_start(modr[:, l, :], a["mod_b"][l].partition_broadcast(2)).then_inc(s_b, 16)
                        act.dma_start(gn[:, l, 0, :], a["norm_mix"][l].partition_broadcast(2)).then_inc(s_b, 16)
                        act.dma_start(gn[:, l, 1, :], a["norm_ffn"][l].partition_broadcast(2)).then_inc(s_b, 16)
                    for l in range(2):
                        with act.Fori(0, NP // STEP) as it:
                            for i in range(STEP):
                                act.wait_ge(w_in[i % RING], (it * (STEP // RING) + l * (NP // RING) + i // RING + 1) * 16)
                                act.wait_ge(s_mm, it * STEP + l * NP + i + 1)
                                nc.scalar.activation(W_hi[:, i % 2], W[:, i % RING], ACT.Copy).then_inc(s_hi, 1)
                    act.wait_ge(s_con, 16)

                @block.tensor
                def _(pe):
                    pe.wait_ge(s_act, 3)
                    pe.sem_inc(s_mm, 2)
                    for l in range(2):
                        with pe.Fori(0, NP // STEP) as it:
                            for i in range(STEP):
                                b = i % 2
                                pe.wait_ge(s_add, it * STEP + l * NP + i + 1)
                                pe.wait_ge(s_hi, it * STEP + l * NP + i + 1)
                                for n, (v, w) in enumerate(((c_hi, W_hi), (c_lo, W_hi), (c_hi, W_lo))):
                                    if n == 2:
                                        pe.wait_ge(s_lo, it * STEP + l * NP + i + 4)
                                    for k in range(KD):
                                        m = nc.tensor.matmul(bank(b)[0:2, :], v[:, :, k], w[:, b, k, :],
                                                             start=n == 0 and k == 0, stop=n == 2 and k == KD - 1)
                                m.then_inc(s_mm, 1)

                @block.vector
                def _(dve):
                    dve.sem_inc(s_add, 2)
                    dve.sem_inc(s_lo, 3)
                    dve.wait_ge(s_act, 2)
                    nc.vector.tensor_tensor(c_lo[:, :, :], cact[:, :, :], c_hi[:, :, :].bitcast(F32), ALU.subtract).then_inc(s_act, 1)

                    def add(it, l, i):
                        dve.wait_ge(s_mm, it * STEP + l * NP + i + 3)
                        dve.wait_ge(s_b, 96)
                        cols = bass.ds((it * STEP + i) * HALF + l * NMOD * D, HALF)
                        flat = modr[:, :, :].rearrange("v l n -> v (l n)")
                        nc.vector.tensor_tensor(flat[:, cols], bank(i % 2)[0:2, :], flat[:, cols], ALU.add).then_inc(s_add, 1)

                    for l in range(2):
                        with dve.Fori(0, NP // STEP) as it:
                            for i in range(STEP):
                                dve.wait_ge(s_hi, it * STEP + l * NP + i + 1)
                                nc.vector.tensor_tensor(W_lo[:, i % 2], W[:, i % RING], W_hi[:, i % 2].bitcast(F32),
                                                        ALU.subtract).then_inc(s_lo, 1)
                                if i:
                                    add(it, l, i - 1)
                            add(it, l, STEP - 1)
                        for n, r in enumerate((1, 4)):
                            dve.wait_ge(s_add, 2 + NP * (l + 1))
                            v = modr[:, l, r * D:(r + 1) * D]
                            nc.vector.scalar_tensor_tensor(out=v, in0=v, scalar=1.0, in1=gn[:, l, n, :],
                                                           op0=ALU.add, op1=ALU.mult).then_inc(s_rows, 1)

                @block.gpsimd
                def _(pool):
                    nc.gpsimd.memset(zero[:, :], 0).then_inc(s_zero, 1)
                    pool.wait_ge(s_zero, 1)
                    for l in range(2):
                        flat = idx_dram[l].rearrange("s n -> (s n)")
                        total = (ITEMS[l] + 1) * CAP[l] * 16
                        per = total // P
                        pool.dma_start(flat.rearrange("(p n) -> p n", p=P), zero[:, 0:per]).then_inc(s_idx, 16)
                    pool.wait_ge(s_idx, 32)

        EARLY = (("q", 0, 512), ("k", 0, 512), ("q", 512, 512), ("k", 512, 512))
        EARLY_BANK = (0, 1, 2, 7)

        def project_chunk(dst, hT, wq, kind, c0, w):
            for k in range(KD):
                m = nc.tensor.matmul(dst, wq[:, 0 if kind == "q" else 1, k, :], hT[:, k, c0:c0 + w],
                                     start=k == 0, stop=k == KD - 1)
            return m

        def load_group(sp, l, g, wq, w_in):
            src = a["w_qkv"][l].rearrange("(k p) n -> p k n", p=P)
            for j in range(3):
                sp.dma_start(wq[:, j], src[:, :, bass.ds(g * P + j * D, P)]).then_inc(w_in, 16)

        def normed(l, mode, T, source, hT=None, rw=None, attn=None, wq=None, w_in=None):
            with ExitStack() as c:
                junk = sb(c, "junk", [P, D])
                hr = sb(c, "hr", [P, 3, D])
                if mode == "ffn":
                    hT = sb(c, "h_tile_T", [P, KD, 2 * P])
                ab = sb(c, "norm_rows", [P, 4, D]) if source == "project" else rows
                s_rows, s_ss, s_rstd, s_sc, s_h, s_g, s_x = (sem(c, n) for n in (
                    "rows_in", "ss_done", "rstd_done", "h_scaled", "h_ready", "branch_gated", "x_added"))
                s_st = [sem(c, f"h_stored{n}") for n in range(3)]
                if source is None:
                    loads = ((0, 2), (2, 5), (5, LT), (LT, NT))
                    s_xin = [sem(c, f"x_in{n}") for n in range(len(loads))]
                    s_toep = sem(c, "toep_out")
                if mode != "final":
                    s_tr, s_eva, s_evd, s_rt, s_rw = (sem(c, n) for n in (
                        "h_transposed", "hT_low", "hT_high", "routed", "router_in"))
                if source == "combine":
                    y = sb(c, "y_pair", [P, 3, 2, D])
                    gate = sb(c, "gate_rows", [P, 2, D])
                    s_gr, s_m, s_c = (sem(c, n) for n in ("gate_rows_in", "y_first", "y_sum"))
                    s_in = [sem(c, f"y_in{n}") for n in range(3)]
                    prev = l - 1 if mode == "mix" else l
                elif source == "project":
                    oT, wo, wo_in = attn
                    tmp = sb(c, "gated", [P, 4, HALF])
                    s_y = sem(c, "y_ready")
                block = c.enter_context(nc.Block())
                B, A = (3, 4) if mode == "ffn" else (0, 1)
                streams = 2 if T > LT else 1
                NROWS = 16 if mode == "final" else 32 * streams
                adds = {"combine": 1, "project": 2, None: 0}[source]
                col = lambda t: slice((t % 2) * P, (t % 2 + 1) * P) if mode == "ffn" else slice(t * P, (t + 1) * P)
                tbank = lambda t: 3 + 2 * (t % 2)
                step_range = range(T + 5)
                at = lambda u, lag: 0 <= u - lag < T
                L_SQ, L_RS, L_SC, L_H, L_TR, L_EV, L_RT = 1, 1, 2, 2, 3, 3, 4

                @block.sync
                def _(sp):
                    if source == "combine":
                        for v in range(streams):
                            sp.dma_start(gate[:, v, :], mods[prev, v, 5 * D:6 * D].partition_broadcast(P)).then_inc(s_gr, 16)
                    if source is None:
                        def load_x(n):
                            t0, t1 = loads[n]
                            src = a["x"][0] if t0 < LT else a["ctx"][0]
                            src = src.rearrange("(t p) d -> p t d", p=P)[:, t0 % LT:(t1 - 1) % LT + 1, :]
                            sp.dma_start(x[:, t0:t1, :], src).then_inc(s_xin[n], 16)

                        load_x(0)
                    if mode == "final":
                        sp.dma_start(ab[:, 0, :], a["final_norm"].partition_broadcast(P)).then_inc(s_rows, 16)
                    else:
                        for v in range(streams):
                            for n, r in enumerate((A, B)):
                                sp.dma_start(ab[:, 2 * v + n, :], mods[l, v, r * D:(r + 1) * D].partition_broadcast(P)).then_inc(s_rows, 16)
                    if mode == "mix" and source == "combine":
                        sp.wait_ge(s_ss, 2)
                        load_group(sp, l, 0, wq, w_in)
                    if source is None:
                        load_x(1)
                        load_group(sp, l, 0, wq, w_in)
                        load_x(2)
                        load_x(3)
                        for h in range(16):
                            src = a["rpb_pad"][h]
                            src = bass.AP(src.tensor, src.offset + GRID_W - 1, [[P, 15], [-1, GRID_W], [1, GRID_W]])
                            sp.dma_start(toep[h].rearrange("q r k -> r q k"), src).then_inc(s_toep, 16)
                        sp.wait_ge(s_toep, 256)
                    if mode == "ffn":
                        sp.dma_start(rw[:, :, :], a["router_w"].rearrange("(k p) e -> p k e", p=P)).then_inc(s_rw, 16)
                    if mode != "mix":
                        for t in range(T):
                            sp.wait_ge(s_h, t + 1)
                            dst = out[0, t * P:(t + 1) * P, :] if mode == "final" else h_dram[t * P:(t + 1) * P, :]
                            sp.dma_start(dst, hr[:, t % 3, :]).then_inc(s_st[t % 3], 16)
                        for n in range(3):
                            sp.wait_ge(s_st[n], 16 * len(range(n, T, 3)))

                @block.tensor
                def _(pe):
                    if source == "project":
                        pe.wait_ge(wo_in, 16 * (4 + streams))
                    if mode == "ffn":
                        pe.wait_ge(s_rw, 16)

                    def project(t):
                        for h in range(2):
                            n = 2 * t + h
                            if n >= 3:
                                pe.wait_ge(s_g, n - 2)
                            for k in range(KD):
                                m = nc.tensor.matmul(bank(n % 3), oT[:, k * NTOK + t * P:k * NTOK + (t + 1) * P],
                                                     wo[:, k, h * HALF:(h + 1) * HALF], start=k == 0, stop=k == KD - 1)
                            m.then_inc(s_y, 1)

                    def transposes(t):
                        pe.wait_ge(s_h, t + 1)
                        if t >= 2:
                            pe.wait_ge(s_eva, t - 1)
                            pe.wait_ge(s_evd, t - 1)
                        for k in range(KD):
                            b = tbank(t) + k // 4
                            m = nc.tensor.transpose(bank(b, (k % 4) * P, (k % 4 + 1) * P), hr[:, t % 3, k * P:(k + 1) * P], ident)
                            if k % 4 == 3:
                                m.then_inc(s_tr, 1)

                    def route(t):
                        pe.wait_ge(s_eva, t + 1)
                        pe.wait_ge(s_evd, t + 1)
                        for k in range(KD):
                            m = nc.tensor.matmul(bank(7, t * NE, (t + 1) * NE), hT[:, k, col(t)], rw[:, k, :],
                                                 start=k == 0, stop=k == KD - 1)
                        m.then_inc(s_rt, 1)

                    for u in step_range:
                        if source == "project" and at(u, 0):
                            project(u)
                        if mode != "final" and at(u, L_TR):
                            transposes(u - L_TR)
                        if mode == "ffn" and at(u, L_RT):
                            route(u - L_RT)
                        if mode == "mix" and u in (8, 9, 12, 13):
                            n = (8, 9, 12, 13).index(u)
                            if n == 0:
                                pe.wait_ge(w_in, 48)
                            pe.wait_ge(s_eva, 4 if n < 2 else 8)
                            pe.wait_ge(s_evd, 4 if n < 2 else 8)
                            project_chunk(bank(EARLY_BANK[n]), hT, wq, *EARLY[n])

                @block.scalar
                def _(act):
                    for u in step_range:
                        if source == "combine" and at(u, 0):
                            act.wait_ge(s_in[u % 3], 32 * (u // 3 + 1))
                            nc.scalar.activation(y[:, u % 3, 0, :], y[:, u % 3, 0, :], ACT.Copy, scale=gates[:, u, 0:1]).then_inc(s_m, 1)
                        if at(u, L_SQ):
                            t = u - L_SQ
                            if t:
                                act.wait_ge(s_ss, t)
                            if source is None:
                                for n, (t0, t1) in enumerate(loads):
                                    if t == t0:
                                        act.wait_ge(s_xin[n], 16)
                            else:
                                act.wait_ge(s_x, adds * (t + 1))
                            nc.scalar.activation(junk[:, :], x[:, t, :], ACT.Square, accum_out=ss[:, t:t + 1]).then_inc(s_ss, 1)
                        if mode != "final" and at(u, L_EV):
                            t = u - L_EV
                            act.wait_ge(s_tr, 2 * t + 1)
                            if mode == "ffn" and t >= 2:
                                act.wait_ge(s_rt, t - 1)
                            nc.scalar.activation(hT[:, 0:4, col(t)], bank(tbank(t)).rearrange("p (k n) -> p k n", n=P),
                                                 ACT.Copy).then_inc(s_eva, 1)

                @block.vector
                def _(dve):
                    if source == "combine":
                        dve.wait_ge(s_gr, 16 * streams)
                    if source == "project":
                        dve.wait_ge(wo_in, 16 * (4 + streams))
                    for u in step_range:
                        if source == "combine" and at(u, 0):
                            y0, y1 = y[:, u % 3, 0, :], y[:, u % 3, 1, :]
                            dve.wait_ge(s_m, u + 1)
                            nc.vector.scalar_tensor_tensor(out=y0, in0=y1, scalar=gates[:, u, 1:2], in1=y0, op0=ALU.mult, op1=ALU.add).then_inc(s_c, 1)
                            dve.wait_ge(s_c, u + 1)
                            nc.vector.tensor_tensor(y0, y0, gate[:, 1 if u >= LT else 0, :], ALU.mult).then_inc(s_g, 1)
                            dve.wait_ge(s_g, u + 1)
                            nc.vector.tensor_tensor(x[:, u, :], x[:, u, :], y0, ALU.add).then_inc(s_x, 1)
                        if source == "project" and at(u, 0):
                            for h in range(2):
                                n = 2 * u + h
                                dve.wait_ge(s_y, n + 1)
                                if n >= 4:
                                    dve.wait_ge(s_x, n - 3)
                                nc.vector.tensor_tensor(tmp[:, n % 4, :], bank(n % 3), rows[:, 2 if u >= LT else 3, h * HALF:(h + 1) * HALF],
                                                        ALU.mult).then_inc(s_g, 1)
                        if at(u, L_SC):
                            t = u - L_SC
                            if t >= 3:
                                if mode != "final":
                                    dve.wait_ge(s_tr, 2 * (t - 3) + 2)
                                if mode != "mix":
                                    dve.wait_ge(s_st[t % 3], 16 * (t // 3))
                            if t == 0:
                                dve.wait_ge(s_rows, NROWS)
                            dve.wait_ge(s_rstd, 2 * t + 2)
                            nc.vector.scalar_tensor_tensor(out=hr[:, t % 3, :], in0=x[:, t, :], scalar=rstd[:, t:t + 1],
                                                           in1=ab[:, 2 * (t >= LT), :], op0=ALU.mult, op1=ALU.mult
                                                           ).then_inc(s_h if mode == "final" else s_sc, 1)
                            if source is None:
                                dve.wait_ge(s_sc, 2 * t + 1)
                                nc.vector.tensor_tensor(hr[:, t % 3, HALF:D], hr[:, t % 3, HALF:D], ab[:, 2 * (t >= LT) + 1, HALF:D],
                                                        ALU.add).then_inc(s_sc, 1)
                        if mode != "final" and at(u, L_EV):
                            t = u - L_EV
                            dve.wait_ge(s_tr, 2 * t + 2)
                            if mode == "ffn" and t >= 2:
                                dve.wait_ge(s_rt, t - 1)
                            nc.vector.tensor_copy(hT[:, 4:8, col(t)], bank(tbank(t) + 1).rearrange("p (k n) -> p k n", n=P)).then_inc(s_evd, 1)

                @block.gpsimd
                def _(pool):
                    def gather(t):
                        if t >= 3:
                            pool.wait_ge(s_x, t - 2)
                        for i in range(2):
                            nc.gpsimd.indirect_dma_start(out=y[:, t % 3, i, :], out_offset=None, in_=ys,
                                                         in_offset=bass.IndirectOffsetOnAxis(slots[:, t, i:i + 1], 0)).then_inc(s_in[t % 3], 16)

                    if source == "combine":
                        gather(0)
                        gather(1)
                    for u in step_range:
                        if source == "combine" and u + 2 < T:
                            gather(u + 2)
                        if source == "project" and at(u, 0):
                            for h in range(2):
                                n = 2 * u + h
                                pool.wait_ge(s_g, n + 1)
                                xs = x[:, u, h * HALF:(h + 1) * HALF]
                                nc.gpsimd.tensor_tensor(xs, xs, tmp[:, n % 4, :], ALU.add).then_inc(s_x, 1)
                        if at(u, L_RS):
                            t = u - L_RS
                            pool.wait_ge(s_ss, t + 1)
                            nc.gpsimd.tensor_scalar(std[:, t:t + 1], ss[:, t:t + 1], 1.0 / D, EPS, ALU.mult, ALU.add).then_inc(s_rstd, 1)
                            pool.wait_ge(s_rstd, 2 * t + 1)
                            nc.gpsimd.tensor_tensor(rstd[:, t:t + 1], std[:, t:t + 1], con[:, C_HALF:C_HALF + 1], ALU.pow).then_inc(s_rstd, 1)
                        if mode != "final" and at(u, L_H):
                            t = u - L_H
                            if t == 0:
                                pool.wait_ge(s_rows, NROWS)
                            pool.wait_ge(s_sc, 2 * t + 2 if source is None else t + 1)
                            w = HALF if source is None else D
                            nc.gpsimd.tensor_tensor(hr[:, t % 3, 0:w], hr[:, t % 3, 0:w], ab[:, 2 * (t >= LT) + 1, 0:w], ALU.add).then_inc(s_h, 1)

        def load_output_weights(sp, l, hT, wo_in):
            wo = a["w_o"][l].rearrange("(k p) n -> p k n", p=P)
            for k in range(0, KD, 2):
                sp.dma_start(hT[:, k:k + 2, 0:D], wo[:, k:k + 2, :]).then_inc(wo_in, 16)
            for v in range(2 if l == 0 else 1):
                sp.dma_start(rows[:, 3 - v, :], mods[l, v, 2 * D:3 * D].partition_broadcast(P)).then_inc(wo_in, 16)

        def neighbourhood(hT, oT, wo_in, wq, w_in):
            with ExitStack() as c:
                qT = sb(c, "na_qT", [P, 2, NTOK])
                kT = sb(c, "na_kT", [P, NTOK])
                V = sb(c, "na_V", [P, NT, P])
                pb = sb(c, "na_probs", [P, 3, 7 * P])
                pT = rows[:, 0:2, 0:7 * P]
                osb = sb(c, "na_out", [P, 2, P])
                mx = sb(c, "na_negmax", [P, 4])
                ls = sb(c, "na_sum", [P, 4])
                rl = sb(c, "na_suminv", [P, 2])
                raw = sb(c, "bias_raw", [P, 2, TABR * GRID_W])
                tin = sb(c, "bias_interior", [P, 2, INTR * GRID_W])
                ted = sb(c, "bias_edge", [P, 2, TABR * GRID_W])
                rest = ys.rearrange("(p n) (b d) -> p (n b) d", p=P, d=HALF)
                CLEARS = -(-rest.shape[1] // 16)
                zeros = rows[:, 3, 0:HALF]
                s_z, s_qz, s_cleared = sem(c, "zeros_set"), sem(c, "na_q_zeros"), sem(c, "slots_cleared")
                s_mm, s_qk, s_v, s_S, s_pre, s_max, s_exp, s_T, s_pT, s_o, s_rl, s_osb, s_oTp, s_oT, s_raw, s_tab = (
                    sem(c, n) for n in ("na_projected", "na_qk_taken", "na_v_taken", "na_scores", "na_biased",
                                        "na_max", "na_exp", "na_transposed", "na_probsT_ready", "na_pv", "na_inverse",
                                        "na_out_taken", "na_outT_psum", "na_outT", "na_bias_in", "na_bias_table"))
                block = c.enter_context(nc.Block())
                steps = [(t, h) for t in range(NT) for h in range(2)]
                NS = len(steps)
                chunks = [*EARLY, ("q", 1024, 256), ("k", 1024, 256),
                          ("v", 0, 4), ("v", 4, 4), ("v", 8, 2)]
                NM, NQK = len(chunks), 6
                chunk_bank = (0, 1, 2, 3, 0, 1, 4, 5, 7)

                def keys(s):
                    k0, n = window(steps[s][0])
                    return list(range(k0, k0 + n)) + list(range(LT, NT))

                def parts(s):
                    k0, n = window(steps[s][0])
                    return {0: [(0, 256, SEQ)], 4: [(0, 512, k0 * P), (512, 256, SEQ)],
                            5: [(0, 512, k0 * P), (512, 128, (k0 + 4) * P), (640, 256, SEQ)]}[n]

                def rounds(s):
                    n = len(keys(s))
                    return [(0, min(n, 4))] + ([(4, n)] if n > 4 else [])

                rb = np.cumsum([0] + [len(rounds(s)) for s in range(NS)]).tolist()
                NR = rb[-1]
                S = lambda s, c0, c1: ps[:, (s % 2) * 2 * HALF + c0:(s % 2) * 2 * HALF + c1]
                O = lambda s: bank(4 if s % 2 == 0 else 7, 0, HD)
                OT = bank(6, 384, 512)

                @block.sync
                def _(sp):
                    tv = toep.rearrange("h q r k -> (h q) (r k)")

                    def load_bias(g):
                        sp.wait_ge(s_tab, g * 4 + 1)
                        for h in range(2):
                            for r in range(2):
                                sp.dma_start(raw[r * GRID_W:(r + 1) * GRID_W, h, :],
                                             tv[bass.ds((g * 2 + h) * GRID_W, GRID_W), (1 - r) * GRID_W:(1 - r + TABR) * GRID_W]).then_inc(s_raw, 16)

                    load_bias(0)
                    with sp.Fori(1, GROUPS) as g:
                        sp.wait_ge(s_mm, g * NM + 1)
                        load_group(sp, 0, g, wq, w_in)
                        load_bias(g)
                    sp.wait_ge(s_mm, GROUPS * NM + 1)
                    sp.wait_ge(s_cleared, CLEARS * 16)
                    load_output_weights(sp, 0, hT, wo_in)

                @block.gpsimd
                def _(pool):
                    pool.sem_inc(s_tab, 1)
                    nc.gpsimd.memset(zeros, 0.0).then_inc(s_z, 1)
                    pool.wait_ge(s_z, 1)
                    for n in range(0, rest.shape[1], 16):
                        m = min(16, rest.shape[1] - n)
                        pool.dma_start(rest[:, n:n + m, :], zeros.unsqueeze(1).to_broadcast([P, m, HALF])).then_inc(s_cleared, 16)
                    with pool.Fori(0, GROUPS) as g:
                        pool.wait_ge(s_raw, (g + 1) * 64)
                        pool.wait_ge(s_pre, g * NS + 1)
                        for h in range(2):
                            v = lambda z, j0, j1: z[:, h, j0 * GRID_W:j1 * GRID_W].rearrange("p (j k) -> p j k", k=GRID_W)
                            nc.gpsimd.tensor_tensor(v(ted, 0, TABR), v(raw, 0, TABR),
                                                    con[:, C_EDGE:C_INT].unsqueeze(1).to_broadcast([P, TABR, GRID_W]), ALU.add).then_inc(s_tab, 1)
                            nc.gpsimd.tensor_tensor(tin[:, h, :], raw[:, h, 2 * GRID_W:(2 + INTR) * GRID_W],
                                                    con[:, C_INT:C_P4], ALU.add).then_inc(s_tab, 1)
                    pool.wait_ge(s_cleared, CLEARS * 16)

                @block.tensor
                def _(pe):
                    pe.sem_inc(s_mm, 1 + len(EARLY))

                    def project(g, n):
                        kind, c0, w = chunks[n]
                        b = chunk_bank[n]
                        if n == 0:
                            pe.wait_ge(w_in, (g + 1) * 48)
                        if 4 <= n < NQK:
                            pe.wait_ge(s_qk, g * NQK + n - 3)
                        if kind == "v":
                            for t in range(w):
                                for k in range(KD):
                                    m = nc.tensor.matmul(bank(b, t * P, (t + 1) * P), hT[:, k, (c0 + t) * P:(c0 + t + 1) * P],
                                                         wq[:, 2, k, :], start=k == 0, stop=k == KD - 1)
                        else:
                            m = project_chunk(bank(b, 0, w), hT, wq, kind, c0, w)
                        m.then_inc(s_mm, 1)

                    for n in range(len(EARLY), NQK):
                        project(0, n)

                    def group(g, last, first=False):
                        def scores(s):
                            t, h = steps[s]
                            if s >= 2:
                                pe.wait_ge(s_pre, g * NS + s)
                            for c0, w, k0 in parts(s):
                                m = nc.tensor.matmul(S(s, c0, c0 + w), qT[:, h, t * P:(t + 1) * P], kT[:, k0:k0 + w], start=True, stop=True)
                            m.then_inc(s_S, 1)

                        def out_transpose(t):
                            pe.wait_ge(s_osb, g * NS + 2 * t + 2)
                            nc.tensor.transpose(OT, osb[:, t % 2, :], ident).then_inc(s_oTp, 1)

                        project(g, NQK)
                        pe.wait_ge(s_qk, g * NQK + NQK)
                        if first:
                            pe.wait_ge(s_qz, 2)
                        scores(0)
                        project(g, NQK + 1)
                        project(g, NQK + 2)
                        scores(1)
                        pe.wait_ge(s_v, g * 3 + 3)
                        if not first:
                            pe.wait_ge(s_oT, g * NT)
                        for s in range(NS):
                            t, h = steps[s]
                            pe.wait_ge(s_exp, g * NS + s + 1)
                            for r, (i0, i1) in enumerate(rounds(s)):
                                if r and h == 0 and t >= 2:
                                    pe.wait_ge(s_oT, g * NT + t - 1)
                                for i in range(i0, i1):
                                    m = nc.tensor.transpose(bank(5 + r, (i - i0) * P, (i - i0 + 1) * P), pb[:, s % 3, i * P:(i + 1) * P], ident)
                                m.then_inc(s_T, 1)
                            if h == 1 and t:
                                if not rounds(s)[1:]:
                                    pe.wait_ge(s_oT, g * NT + t - 1)
                                out_transpose(t - 1)
                            if s + 2 < NS:
                                scores(s + 2)
                            pe.wait_ge(s_pT, g * NR + rb[s + 1])
                            if s >= 2:
                                pe.wait_ge(s_osb, g * NS + s - 1)
                            ks = keys(s)
                            for i, kt in enumerate(ks):
                                m = nc.tensor.matmul(O(s), pT[:, s % 2, i * P:(i + 1) * P], V[:, kt, h * HD:(h + 1) * HD],
                                                     start=i == 0, stop=i == len(ks) - 1)
                            m.then_inc(s_o, 1)
                            if s == NS - 2 and not last:
                                pe.wait_ge(s_pre, (g + 1) * NS + 1)
                                project(g + 1, 0)
                                project(g + 1, 1)
                        if not last:
                            for n in range(2, NQK):
                                project(g + 1, n)
                        pe.wait_ge(s_oT, g * NT + NT - 1)
                        out_transpose(NT - 1)

                    group(0, False, first=True)
                    with pe.Fori(1, GROUPS - 1) as g:
                        group(g, False)
                    group(GROUPS - 1, True)

                @block.vector
                def _(dve):
                    dve.sem_inc(s_pre, 1)
                    nc.vector.memset(qT[HD:P, 0, :], 0.0).then_inc(s_qz, 1)
                    nc.vector.memset(qT[0:HD, 1, :], 0.0).then_inc(s_qz, 1)
                    with dve.Fori(0, GROUPS) as g:
                        def take_values(n):
                            kind, t0, w = chunks[NQK + n]
                            dve.wait_ge(s_mm, g * NM + NQK + n + 2)
                            nc.vector.tensor_copy(V[:, t0:t0 + w, :], bank(chunk_bank[NQK + n], 0, w * P).rearrange("p (t n) -> p t n", n=P)).then_inc(s_v, 1)

                        take_values(0)
                        dve.wait_ge(s_tab, (g + 1) * 4 + 1)

                        def soft(s):
                            t, h = steps[s]
                            k0, n = window(t)
                            dve.wait_ge(s_S, g * NS + s + 1)
                            if s >= 3:
                                dve.wait_ge(s_T, g * NR + rb[s - 2])
                            w = n * P
                            if n:
                                j0 = 2 * k0 - 2 * t + 6
                                bias = tin[:, h, :] if n == 5 else ted[:, h, j0 * GRID_W:(j0 + WIN_ROWS) * GRID_W]
                                nc.vector.tensor_tensor(pb[:, s % 3, 0:w], S(s, 0, w), bias, ALU.add).then_inc(s_rl, 1)
                            else:
                                dve.sem_inc(s_rl, 1)
                            nc.vector.tensor_copy(pb[:, s % 3, w:w + CTX], S(s, w, w + CTX)).then_inc(s_pre, 1)
                            dve.wait_ge(s_rl, g * 2 * NS + rln(s))
                            dve.wait_ge(s_pre, g * NS + s + 2)
                            nc.vector.tensor_reduce(mx[:, s % 4:s % 4 + 1], pb[:, s % 3, 0:w + CTX], AX.X, ALU.max, negate=True).then_inc(s_max, 1)

                        def rln(s):
                            return s + 1 + max(0, s - 2)

                        def take(s):
                            t, h = steps[s]
                            dve.wait_ge(s_o, g * NS + s + 1)
                            nc.vector.reciprocal(rl[:, s % 2:s % 2 + 1], ls[:, s % 4:s % 4 + 1]).then_inc(s_rl, 1)
                            dve.wait_ge(s_rl, g * 2 * NS + min(s + 3, NS) + s + 1)
                            if h == 0 and t >= 2:
                                dve.wait_ge(s_oTp, g * NT + t - 1)
                            nc.vector.tensor_scalar(osb[:, t % 2, h * HD:(h + 1) * HD], O(s), rl[:, s % 2:s % 2 + 1], None, ALU.mult).then_inc(s_osb, 1)

                        soft(0)
                        take_values(1)
                        take_values(2)
                        soft(1)
                        for s in range(NS):
                            if s + 2 < NS:
                                soft(s + 2)
                            take(s)

                @block.scalar
                def _(act):

                    def take(g, n, early=False):
                        kind, c0, w = chunks[n]
                        act.wait_ge(s_mm, g * NM + n + 2)
                        b = EARLY_BANK[n] if early else chunk_bank[n]
                        if kind == "q":
                            nc.scalar.activation(qT[0:HD, 0, c0:c0 + w], bank(b, 0, w)[0:HD], ACT.Copy, scale=SCALE)
                            nc.scalar.activation(qT[HD:P, 1, c0:c0 + w], bank(b, 0, w)[HD:P], ACT.Copy, scale=SCALE).then_inc(s_qk, 1)
                        else:
                            nc.scalar.activation(kT[:, c0:c0 + w], bank(b, 0, w), ACT.Copy).then_inc(s_qk, 1)

                    for n in range(NQK):
                        take(0, n, early=n < len(EARLY))

                    def group(g, last):

                        def exp(s):
                            w = len(keys(s)) * P
                            act.wait_ge(s_max, g * NS + s + 1)
                            nc.scalar.activation(pb[:, s % 3, 0:w], pb[:, s % 3, 0:w], ACT.Exp, bias=mx[:, s % 4:s % 4 + 1],
                                                 accum_out=ls[:, s % 4:s % 4 + 1]).then_inc(s_exp, 1)

                        def outT(t):
                            act.wait_ge(s_oTp, g * NT + t + 1)
                            nc.scalar.activation(oT[:, bass.ds(g * NTOK + t * P, P)], OT, ACT.Copy).then_inc(s_oT, 1)

                        exp(0)
                        for s in range(NS):
                            t, h = steps[s]
                            for r, (i0, i1) in enumerate(rounds(s)):
                                act.wait_ge(s_T, g * NR + rb[s] + r + 1)
                                if r and h == 1 and t:
                                    act.wait_ge(s_oTp, g * NT + t)
                                nc.scalar.activation(pT[:, s % 2, i0 * P:i1 * P], bank(5 + r, 0, (i1 - i0) * P), ACT.Copy).then_inc(s_pT, 1)
                            if h == 1 and t:
                                outT(t - 1)
                            if s + 1 < NS:
                                exp(s + 1)
                            if s == NS - 2 and not last:
                                take(g + 1, 0)
                                take(g + 1, 1)
                        if not last:
                            for n in range(2, NQK):
                                take(g + 1, n)
                        outT(NT - 1)

                    with act.Fori(0, GROUPS - 1) as g:
                        group(g, False)
                    group(GROUPS - 1, True)

        def differential(hT, oT, wo_in, wq, w_in):
            with ExitStack() as c:
                qT = sb(c, "df_qT", [P, SEQ])
                kT = sb(c, "df_kT", [P, NTOK])
                V = sb(c, "df_V", [P, NT, P])
                rq = sb(c, "df_raw_qk", [P, 2, SEQ])
                trig = sb(c, "trig", [P, 2, SEQ])
                pb = sb(c, "df_probs", [P, 3, NTOK])
                pT = rows[:, :, :].rearrange("p r d -> p (r d)")[:, 0:2 * NTOK].rearrange("p (b n) -> p b n", b=2)
                mx = sb(c, "df_negmax", [P, 4])
                ls = sb(c, "df_sum", [P, 4])
                rl = sb(c, "df_suminv", [P, 4])
                cf = sb(c, "df_weight", [P, 2])
                lam = sb(c, "lam", [P, 4, HD])
                lamt = sb(c, "lamt", [P, 2, HD])
                lams = sb(c, "lams", [P, 6])
                gsub = sb(c, "gsub", [P, 1])
                oraw = sb(c, "df_out", [P, 2, P])
                osq = sb(c, "df_square", [P, P])
                oss = sb(c, "df_sumsq", [P, 3])
                osb = sb(c, "df_normed", [P, 2, P])
                s_mm, s_qk, s_v, s_S, s_max, s_exp, s_T, s_pT, s_o, s_cf, s_dif, s_on, s_osb, s_oTp, s_oT, s_rop, s_sin, s_cos, s_rot, s_lin, s_lam, s_half = (
                    sem(c, n) for n in ("df_projected", "df_qk_taken", "df_v_taken", "df_scores", "df_max", "df_exp",
                                        "df_transposed", "df_probsT_ready", "df_pv", "df_weight_steps", "df_combined", "df_norm_steps",
                                        "df_out_ready", "df_outT_psum", "df_outT", "df_partner", "df_sin", "df_cos", "df_rotated",
                                        "df_consts_in", "lambda_steps", "df_map0_scored"))
                block = c.enter_context(nc.Block())
                chunks = [*EARLY, ("k", 1024, 256),
                          ("v", 0, 4), ("v", 4, 4), ("v", 8, 2)]
                NM, NQK, NROT = len(chunks), 5, 4
                parts = (((0, 0, 512), (512, 512, 512), (SEQ, SEQ, CTX)),
                         ((NTOK, SEQ, CTX), (NTOK + CTX, 0, 512), (NTOK + CTX + 512, 512, 512)))
                S = lambda m: ps[:, m * NTOK:(m + 1) * NTOK]
                rounds = ((0, 4), (4, 8), (8, NT))
                NR = len(rounds)
                TB = lambda r: 5 + r % 2
                O = bank(7, 0, P)
                OT = bank(6, 0, P)
                rot = lambda r: (r % 2, slice((r // 2) * 512, (r // 2) * 512 + 512))

                @block.sync
                def _(sp):
                    sp.dma_start(trig[:, :, :], a["trig"].rearrange("p (a n) -> p a n", a=2)).then_inc(s_lin, 16)
                    sp.dma_start(lam[:, :, :], a["diff_lambda"][0].rearrange("a d -> (a d)").partition_broadcast(P)
                                 .rearrange("p (a d) -> p a d", a=4)).then_inc(s_lin, 16)
                    sp.dma_start(gsub[:, :], a["diff_subln"][0].rearrange("(p a) -> p a", a=1)).then_inc(s_lin, 16)
                    with sp.Fori(1, GROUPS) as g:
                        sp.wait_ge(s_mm, g * NM + 1)
                        load_group(sp, 1, g, wq, w_in)
                    sp.wait_ge(s_mm, GROUPS * NM + 1)
                    load_output_weights(sp, 1, hT, wo_in)

                @block.gpsimd
                def _(pool):
                    pool.wait_ge(s_lin, 48)
                    with pool.Fori(0, GROUPS) as g:
                        for r in range(NROT):
                            i, cols = rot(r)
                            pool.wait_ge(s_rop, g * NROT + r + 1)
                            nc.gpsimd.tensor_tensor(rq[:, i, cols], rq[:, i, cols], trig[:, 0, cols], ALU.mult).then_inc(s_cos, 1)
                        for t in range(LT):
                            pool.wait_ge(s_on, g * 4 * LT + 4 * t + 3)
                            nc.gpsimd.tensor_tensor(oss[:, 2:3], oss[:, 1:2], con[:, C_HALF:C_HALF + 1], ALU.pow).then_inc(s_on, 1)

                @block.tensor
                def _(pe):
                    pe.sem_inc(s_mm, 1 + len(EARLY))

                    def project(g, n):
                        kind, c0, w = chunks[n]
                        if n == 0:
                            pe.wait_ge(w_in, (g + 1) * 48)
                        if kind == "v":
                            for t in range(w):
                                for k in range(KD):
                                    m = nc.tensor.matmul(bank(n, t * P, (t + 1) * P), hT[:, k, (c0 + t) * P:(c0 + t + 1) * P],
                                                         wq[:, 2, k, :], start=k == 0, stop=k == KD - 1)
                        else:
                            m = project_chunk(bank(n, 0, w), hT, wq, kind, c0, w)
                        m.then_inc(s_mm, 1)

                    for n in range(len(EARLY), NQK):
                        project(0, n)

                    def group(g, last, first=False):
                        for r in range(NROT):
                            i, cols = rot(r)
                            pe.wait_ge(s_qk, g * NQK + r + 1)
                            nc.tensor.matmul(bank(r), con[:, C_PERM:C_PERM + P], rq[:, i, cols],
                                             start=True, stop=True).then_inc(s_rop, 1)

                        def scores(t, m, which):
                            r = slice(m * HD, (m + 1) * HD)
                            for n in which:
                                c0, k0, w = parts[m][n]
                                mm = nc.tensor.matmul(ps[:, c0:c0 + w], qT[r, t * P:(t + 1) * P], kT[r, k0:k0 + w], start=True, stop=True)
                            return mm

                        def scores_first(t):
                            if t:
                                pe.wait_ge(s_exp, g * 2 * LT + 2 * t - 1)
                            scores(t, 0, (0,))

                        def scores_rest(t):
                            if t:
                                pe.wait_ge(s_exp, g * 2 * LT + 2 * t)
                            scores(t, 0, (2,)).then_inc(s_half, 1)
                            scores(t, 0, (1,))
                            pe.wait_ge(s_half, g * LT + t + 1)
                            scores(t, 1, (0,)).then_inc(s_S, 1)
                            scores(t, 1, (1, 2)).then_inc(s_S, 1)

                        def transposes(t, r):
                            if r == 1 and t >= 2:
                                pe.wait_ge(s_oT, g * LT + t - 1)
                            if r == 2:
                                pe.wait_ge(s_pT, g * LT * NR + t * NR + 1)
                            i0, i1 = rounds[r]
                            for i in range(i0, i1):
                                mm = nc.tensor.transpose(bank(TB(r), (i - i0) * P, (i - i0 + 1) * P), pb[:, t % 2, i * P:(i + 1) * P], ident)
                            mm.then_inc(s_T, 1)

                        def pv(t, r):
                            pe.wait_ge(s_pT, g * LT * NR + t * NR + r + 1)
                            if r == 0 and t:
                                pe.wait_ge(s_on, g * 4 * LT + 4 * t - 3)
                            for i in range(*rounds[r]):
                                mm = nc.tensor.matmul(O, pT[:, t % 2, i * P:(i + 1) * P], V[:, i, :], start=i == 0, stop=i == NT - 1)
                            if r == NR - 1:
                                mm.then_inc(s_o, 1)

                        def out_transpose(t):
                            pe.wait_ge(s_osb, g * LT + t + 1)
                            if t == LT - 1:
                                pe.wait_ge(s_oT, g * LT + t)
                            nc.tensor.transpose(OT, osb[:, t % 2, :], ident).then_inc(s_oTp, 1)

                        project(g, NQK)
                        pe.wait_ge(s_rot, g * NROT + NROT)
                        pe.wait_ge(s_qk, g * NQK + NQK)
                        scores_first(0)
                        scores_rest(0)
                        if not first:
                            pe.wait_ge(s_oT, g * LT)
                        project(g, NQK + 1)
                        project(g, NQK + 2)
                        scores_first(1)
                        scores_rest(1)
                        pe.wait_ge(s_v, g * 3 + 3)
                        for t in range(LT):
                            pe.wait_ge(s_dif, g * LT + t + 1)
                            transposes(t, 0)
                            transposes(t, 1)
                            pv(t, 0)
                            transposes(t, 2)
                            pv(t, 1)
                            pv(t, 2)
                            if t:
                                out_transpose(t - 1)
                            if t + 2 < LT:
                                scores_first(t + 2)
                                scores_rest(t + 2)
                            if t == LT - 2 and not last:
                                pe.wait_ge(s_exp, (g + 1) * (2 * LT))
                                project(g + 1, 0)
                                project(g + 1, 1)
                        if not last:
                            for n in range(2, NQK):
                                project(g + 1, n)
                        out_transpose(LT - 1)

                    group(0, False, first=True)
                    with pe.Fori(1, GROUPS - 1) as g:
                        group(g, False)
                    group(GROUPS - 1, True)

                @block.scalar
                def _(act):
                    act.wait_ge(s_lam, 2)
                    nc.scalar.activation(lams[:, 2:4], lams[:, 0:2], ACT.Exp).then_inc(s_lam, 1)

                    def take(g, n, early=False):
                        kind, c0, w = chunks[n]
                        act.wait_ge(s_mm, g * NM + n + 2)
                        dst = kT[:, c0:c0 + w] if c0 >= SEQ else rq[:, 0 if kind == "q" else 1, c0:c0 + w]
                        b = EARLY_BANK[n] if early else n
                        nc.scalar.activation(dst, bank(b, 0, w), ACT.Copy, scale=SCALE if kind == "q" else 1.0).then_inc(s_qk, 1)

                    for n in range(NQK):
                        take(0, n, early=n < len(EARLY))

                    def group(g, last):

                        def exp(t, m):
                            act.wait_ge(s_max, g * 2 * LT + 2 * t + 2)
                            if m == 1 and t:
                                act.wait_ge(s_dif, g * LT + t)
                            if m == 0 and t >= 2:
                                act.wait_ge(s_T, g * LT * NR + (t - 1) * NR)
                            nc.scalar.activation(pb[:, t % 2 if m == 0 else 2, :], S(m), ACT.Exp,
                                                 bias=mx[:, 2 * (t % 2) + m:2 * (t % 2) + m + 1],
                                                 accum_out=ls[:, 2 * (t % 2) + m:2 * (t % 2) + m + 1]).then_inc(s_exp, 1)

                        def outT(t):
                            act.wait_ge(s_oTp, g * LT + t + 1)
                            act.wait_ge(s_lam, 6)
                            nc.scalar.activation(oT[:, bass.ds(g * NTOK + t * P, P)], OT, ACT.Copy, scale=gsub[:, 0:1]).then_inc(s_oT, 1)

                        def take_probs(t, r):
                            i0, i1 = rounds[r]
                            act.wait_ge(s_T, g * LT * NR + t * NR + r + 1)
                            nc.scalar.activation(pT[:, t % 2, i0 * P:i1 * P], bank(TB(r), 0, (i1 - i0) * P), ACT.Copy).then_inc(s_pT, 1)

                        exp(0, 0)
                        exp(0, 1)
                        for t in range(LT):
                            take_probs(t, 0)
                            take_probs(t, 1)
                            if t + 1 < LT:
                                exp(t + 1, 0)
                            take_probs(t, 2)
                            if t + 1 < LT:
                                exp(t + 1, 1)
                            if t:
                                outT(t - 1)
                            if t == LT - 2 and not last:
                                take(g + 1, 0)
                                take(g + 1, 1)
                        if not last:
                            for n in range(2, NQK):
                                take(g + 1, n)
                        outT(LT - 1)

                    with act.Fori(0, GROUPS - 1) as g:
                        group(g, False)
                    group(GROUPS - 1, True)

                @block.vector
                def _(dve):
                    dve.wait_ge(s_lin, 48)
                    for n in range(2):
                        nc.vector.tensor_tensor_reduce(out=lamt[:, n, :], in0=lam[:, 2 * n, :], in1=lam[:, 2 * n + 1, :],
                                                       scale=1.0, scalar=0.0, op0=ALU.mult, op1=ALU.add,
                                                       accum_out=lams[:, n:n + 1]).then_inc(s_lam, 1)
                    dve.wait_ge(s_lam, 3)
                    nc.vector.tensor_tensor(lams[:, 4:5], lams[:, 2:3], lams[:, 3:4], ALU.subtract).then_inc(s_lam, 1)
                    dve.wait_ge(s_lam, 4)
                    nc.vector.tensor_scalar(lams[:, 5:6], lams[:, 4:5], LAM_INIT, -1.0, ALU.add, ALU.mult).then_inc(s_lam, 1)
                    nc.vector.tensor_scalar(gsub[:, :], gsub[:, :], 1.0 - LAM_INIT, None, ALU.mult).then_inc(s_lam, 1)
                    dve.wait_ge(s_lam, 6)
                    with dve.Fori(0, GROUPS) as g:
                        def take_values(n):
                            kind, t0, w = chunks[NQK + n]
                            dve.wait_ge(s_mm, g * NM + NQK + n + 2)
                            nc.vector.tensor_copy(V[:, t0:t0 + w, :], bank(NQK + n, 0, w * P).rearrange("p (t n) -> p t n", n=P)).then_inc(s_v, 1)

                        for r in range(NROT):
                            i, cols = rot(r)
                            dst = (qT, kT)[i][:, cols]
                            dve.wait_ge(s_rop, g * NROT + r + 1)
                            nc.vector.tensor_tensor(dst, bank(r), trig[:, 1, cols], ALU.mult).then_inc(s_sin, 1)
                            dve.wait_ge(s_sin, g * NROT + r + 1)
                            dve.wait_ge(s_cos, g * NROT + r + 1)
                            nc.vector.tensor_tensor(dst, dst, rq[:, i, cols], ALU.add).then_inc(s_rot, 1)

                        def mxcol(t, m):
                            return slice(2 * (t % 2) + m, 2 * (t % 2) + m + 1)

                        def maximum(t, m):
                            dve.wait_ge(s_S, g * 2 * LT + 2 * t + m + 1)
                            nc.vector.tensor_reduce(mx[:, mxcol(t, m)], S(m), AX.X, ALU.max, negate=True).then_inc(s_max, 1)

                        def combine(t):
                            dve.wait_ge(s_exp, g * 2 * LT + 2 * t + 2)
                            two = slice(2 * (t % 2), 2 * (t % 2) + 2)
                            nc.vector.reciprocal(rl[:, two], ls[:, two]).then_inc(s_cf, 1)
                            dve.wait_ge(s_cf, g * 2 * LT + 2 * t + 1)
                            nc.vector.scalar_tensor_tensor(out=cf[:, t % 2:t % 2 + 1], in0=ls[:, mxcol(t, 0)], scalar=rl[:, mxcol(t, 1)],
                                                           in1=lams[:, 5:6], op0=ALU.mult, op1=ALU.mult).then_inc(s_cf, 1)
                            dve.wait_ge(s_cf, g * 2 * LT + 2 * t + 2)
                            for dst, src in ((slice(SEQ, NTOK), slice(0, CTX)), (slice(0, SEQ), slice(CTX, NTOK))):
                                last = nc.vector.scalar_tensor_tensor(out=pb[:, t % 2, dst], in0=pb[:, 2, src], scalar=cf[:, t % 2:t % 2 + 1],
                                                                      in1=pb[:, t % 2, dst], op0=ALU.mult, op1=ALU.add)
                            last.then_inc(s_dif, 1)

                        def finish(t):
                            dve.wait_ge(s_o, g * LT + t + 1)
                            nc.vector.tensor_scalar(oraw[:, t % 2, :], O, rl[:, mxcol(t, 0)], None, ALU.mult).then_inc(s_on, 1)

                        def normalise(t):
                            base = g * 4 * LT + 4 * t
                            dve.wait_ge(s_on, base + 1)
                            nc.vector.tensor_tensor_reduce(out=osq[:, :], in0=oraw[:, t % 2, :], in1=oraw[:, t % 2, :], scale=1.0,
                                                           scalar=0.0, op0=ALU.mult, op1=ALU.add, accum_out=oss[:, 0:1]).then_inc(s_on, 1)
                            dve.wait_ge(s_on, base + 2)
                            nc.vector.tensor_scalar(oss[:, 1:2], oss[:, 0:1], 1.0 / P, EPS, ALU.mult, ALU.add).then_inc(s_on, 1)

                        def scale_out(t):
                            dve.wait_ge(s_on, g * 4 * LT + 4 * t + 4)
                            if t >= 2:
                                dve.wait_ge(s_oTp, g * LT + t - 1)
                            nc.vector.tensor_scalar(osb[:, t % 2, :], oraw[:, t % 2, :], oss[:, 2:3], None, ALU.mult).then_inc(s_osb, 1)

                        take_values(0)
                        maximum(0, 0)
                        maximum(0, 1)
                        take_values(1)
                        combine(0)
                        take_values(2)
                        for t in range(LT):
                            if t + 1 < LT:
                                maximum(t + 1, 0)
                                maximum(t + 1, 1)
                            if t:
                                scale_out(t - 1)
                            finish(t)
                            if t + 1 < LT:
                                combine(t + 1)
                            normalise(t)
                        scale_out(LT - 1)

        def load_piece(sp, l, ring, p_in, e, q):
            part = lambda n: a[n].rearrange("l e d f -> (l e d) f")[bass.ds((e + l * NE) * D, D), :].rearrange("(k p) f -> p k f", p=P)
            if q < 4:
                sp.dma_start(ring[:, q, :, 0:256], part("expert_w_gate")[:, :, q * 256:(q + 1) * 256]).then_inc(p_in[q], 16)
                sp.dma_start(ring[:, q, :, 256:512], part("expert_w_up")[:, :, q * 256:(q + 1) * 256]).then_inc(p_in[q], 16)
            else:
                sp.dma_start(ring[:, q], part("expert_w_down")[:, :, (q - 4) * HALF:(q - 3) * HALF]).then_inc(p_in[q], 16)

        def routing(l, ring, p_in):
            T = TILES[l]
            C = CAP[l]
            W = T * NE
            with ExitStack() as c:
                r = lambda name, n, dt=F32: sb(c, name, [P, n], dt)
                sc, sel, msel, w16, oh1, oh2, ohs, cum, pos, t16 = (r(n, W) for n in (
                    "rt_scores", "rt_sel", "rt_masked", "rt_w16", "rt_first", "rt_second", "rt_chosen", "rt_before", "rt_pos", "rt_t16"))
                hi, lo, g4a, g4b, gw = (r(n, T * NG * 2) for n in ("rt_hi", "rt_lo", "rt_g4a", "rt_g4b", "rt_gw"))
                t1, gt, s2 = r("rt_t1", T), r("rt_gt", T * 2), r("rt_s2", T * 2)
                rb = r("rt_bias", NE)
                tot, nch, cend, cbuf, base = (r(n, NE) for n in ("rt_total", "rt_chunks", "rt_end", "rt_endb", "rt_base"))
                cmpb = r("rt_compare", NE * 16)
                tab = r("rt_table", 64)
                cmpt = r("rt_compare_items", 64 * NE)
                slotf = r("rt_slotf", T * 2)
                tok = sb(c, "rt_tok", [P, NT, 16], I32)
                s_in, s_sig, s_ch, s_cnt, s_pos, s_tok, s_tab, s_slot = (sem(c, n) for n in (
                    "rt_in", "rt_sigmoid", "rt_chain", "rt_counted", "rt_ranked", "rt_tok_in", "rt_table_done", "rt_scattered"))
                block = c.enter_context(nc.Block())
                bc = lambda ap, shape: ap.to_broadcast(shape)
                CH_OH, CH_SLOT = [0], [0]

                @block.sync
                def _(sp):
                    sp.dma_start(rb[:, :], a["router_b"].partition_broadcast(P)).then_inc(s_in, 16)
                    sp.dma_start(tok[:, :, :], a["tokens"]).then_inc(s_tok, 16)
                    for q in range(6):
                        load_piece(sp, l, ring, p_in, 0, q)

                @block.scalar
                def _(act):
                    nc.scalar.activation(sc[:, :], bank(7, 0, W), ACT.Sigmoid).then_inc(s_sig, 1)

                @block.vector
                def _(dve):
                    ch = Steps(dve, s_ch)
                    v = nc.vector
                    TE = lambda z: z[:, 0:W].rearrange("p (t e) -> p t e", e=NE)
                    TGE = lambda z: z[:, 0:W].rearrange("p (t g e) -> p t g e", g=NG, e=EPG)
                    TG = lambda z: z[:, 0:T * NG].rearrange("p (t g) -> p t g", g=NG)
                    TG2 = lambda z: z[:, 0:T * NG * 2].rearrange("p (t g b) -> p t g b", g=NG, b=2)
                    pair = lambda z, i: z[:, 0:W].rearrange("p (t g b i) -> p t g b i", g=NG, b=2, i=2)[:, :, :, :, i]
                    dve.wait_ge(s_in, 16)
                    dve.wait_ge(s_sig, 1)
                    ch.then(v.tensor_tensor(TE(sel), TE(sc), bc(rb[:, :].unsqueeze(1), [P, T, NE]), ALU.add))
                    flat_pairs = sel[:, :].rearrange("p (n i) -> p n i", i=2)
                    v.tensor_tensor(lo[:, 0:W // 2], flat_pairs[:, :, 0], flat_pairs[:, :, 1], ALU.min)
                    ch.then(v.tensor_tensor(hi[:, 0:W // 2], flat_pairs[:, :, 0], flat_pairs[:, :, 1], ALU.max))
                    h2 = hi[:, 0:W // 2].rearrange("p (n i) -> p n i", i=2)
                    l2 = lo[:, 0:W // 2].rearrange("p (n i) -> p n i", i=2)
                    N4 = T * NG
                    v.tensor_tensor(g4a[:, 0:N4], h2[:, :, 0], h2[:, :, 1], ALU.max)
                    v.tensor_tensor(g4b[:, 0:N4], h2[:, :, 0], h2[:, :, 1], ALU.min)
                    ch.then(v.tensor_tensor(gw[:, 0:N4], l2[:, :, 0], l2[:, :, 1], ALU.max))
                    ch.then(v.tensor_tensor(g4b[:, 0:N4], g4b[:, 0:N4], gw[:, 0:N4], ALU.max))
                    ch.then(v.tensor_tensor(g4a[:, 0:N4], g4a[:, 0:N4], g4b[:, 0:N4], ALU.add))

                    def first_of_max(dst, src, n, prio):
                        vv = lambda z: z[:, 0:T * n].rearrange("p (t e) -> p t e", e=n)
                        ch.then(v.tensor_reduce(t1[:, :], vv(src), AX.X, ALU.max))
                        ch.then(v.tensor_tensor(vv(dst), vv(src), bc(t1[:, :].unsqueeze(2), [P, T, n]), ALU.is_equal))
                        ch.then(v.tensor_tensor(vv(dst), vv(dst), bc(prio.unsqueeze(1), [P, T, n]), ALU.mult))
                        ch.then(v.tensor_reduce(t1[:, :], vv(dst), AX.X, ALU.max))
                        ch.then(v.tensor_tensor(vv(dst), vv(dst), bc(t1[:, :].unsqueeze(2), [P, T, n]), ALU.is_equal))

                    first_of_max(gw, g4a, NG, con[:, C_P4:C_P16])
                    ch.then(v.tensor_scalar(g4b[:, 0:N4], gw[:, 0:N4], -1.0, -NEG, ALU.add, ALU.mult))
                    gsel = bc(gw[:, 0:N4].rearrange("p (n i) -> p n i", i=1), [P, N4, EPG])
                    goff = bc(g4b[:, 0:N4].rearrange("p (n i) -> p n i", i=1), [P, N4, EPG])
                    n4 = lambda z: z[:, :].rearrange("p (n e) -> p n e", e=EPG)
                    ch.then(v.tensor_tensor(n4(msel), n4(sel), gsel, ALU.mult))
                    ch.then(v.tensor_tensor(n4(msel), n4(msel), goff, ALU.add))
                    first_of_max(oh1, msel, NE, con[:, C_P16:C_THR])
                    ch.then(v.scalar_tensor_tensor(out=msel[:, :], in0=oh1[:, :], scalar=NEG, in1=msel[:, :], op0=ALU.mult, op1=ALU.add))
                    first_of_max(oh2, msel, NE, con[:, C_P16:C_THR])
                    ch.then(v.tensor_tensor(ohs[:, :], oh1[:, :], oh2[:, :], ALU.add))
                    ch.then(v.memset(cum[:, 0:NE], 0.0))
                    for t in range(1, T):
                        ch.then(v.tensor_tensor(cum[:, t * NE:(t + 1) * NE], cum[:, (t - 1) * NE:t * NE], ohs[:, (t - 1) * NE:t * NE], ALU.add))
                    ch.then(v.tensor_tensor(tot[:, :], cum[:, (T - 1) * NE:], ohs[:, (T - 1) * NE:], ALU.add))
                    CH_OH[0] = ch.n
                    dve.wait_ge(s_cnt, 1)
                    ch.then(v.tensor_scalar(tot[:, :], bank(6, 256, 256 + NE), 1.0 / C, None, ALU.mult))
                    c3 = cmpb[:, :].rearrange("p (e j) -> p e j", j=16)
                    ch.then(v.tensor_tensor(c3, bc(tot[:, :].unsqueeze(2), [P, NE, 16]), bc(con[:, C_THR:C_IOTA].unsqueeze(1), [P, NE, 16]), ALU.is_gt))
                    ch.then(v.tensor_reduce(nch[:, :], c3, AX.X, ALU.add))
                    ch.then(v.tensor_scalar(cend[:, :], nch[:, :], 1.0, None, ALU.add))
                    src, dst = cend, cbuf
                    ch.then(v.tensor_copy(nch[:, :], cend[:, :]))
                    for k in (1, 2, 4, 8):
                        ch.then(v.tensor_copy(dst[:, 0:k], src[:, 0:k]))
                        ch.then(v.tensor_tensor(dst[:, k:], src[:, k:], src[:, 0:NE - k], ALU.add))
                        src, dst = dst, src
                    ch.then(v.tensor_tensor(base[:, :], src[:, :], nch[:, :], ALU.subtract))
                    ch.then(v.tensor_scalar(base[:, :], base[:, :], float(C), None, ALU.mult))
                    dve.wait_ge(s_pos, 1)
                    ch.then(v.tensor_tensor(TE(pos), bank(6, 0, W).rearrange("p (t e) -> p t e", e=NE), bc(base[:, :].unsqueeze(1), [P, T, NE]), ALU.add))
                    for i, oh in enumerate((oh1, oh2)):
                        ch.then(v.tensor_tensor(t16[:, :], pos[:, :], oh[:, :], ALU.mult))
                        ch.then(v.tensor_reduce(slotf[:, i * T:(i + 1) * T], TE(t16), AX.X, ALU.add))
                        ch.then(v.tensor_copy(slots[:, 0:T, i], slotf[:, i * T:(i + 1) * T]))
                    CH_SLOT[0] = ch.n
                    ch.then(v.tensor_copy(nitem[:, :], src[:, NE - 1:NE]))
                    i3 = cmpt[:, :].rearrange("p (i e) -> p i e", e=NE)
                    ch.then(v.tensor_tensor(i3, bc(con[:, C_IOTA:C_HALF].unsqueeze(2), [P, 64, NE]), bc(src[:, :].unsqueeze(1), [P, 64, NE]), ALU.is_ge))
                    ch.then(v.tensor_reduce(tab[:, :], i3, AX.X, ALU.add))
                    ch.then(v.tensor_scalar(table[:, :], tab[:, :], float(NE - 1), None, ALU.min))
                    for i, oh in enumerate((oh1, oh2)):
                        ch.then(v.tensor_tensor(t16[:, :], sc[:, :], oh[:, :], ALU.mult))
                        ch.then(v.tensor_reduce(gt[:, i * T:(i + 1) * T], TE(t16), AX.X, ALU.add))
                    ch.then(v.tensor_tensor(t1[:, :], gt[:, 0:T], gt[:, T:2 * T], ALU.add))
                    ch.then(v.reciprocal(t1[:, :], t1[:, :]))
                    for i in range(2):
                        ch.then(v.tensor_tensor(gates[:, 0:T, i], gt[:, i * T:(i + 1) * T], t1[:, :], ALU.mult))

                @block.tensor
                def _(pe):
                    pe.wait_ge(s_ch, CH_OH[0])
                    nc.tensor.matmul(bank(6, 0, W), con[:, C_TRI:C_TRI + P], ohs[:, :], start=True, stop=False)
                    nc.tensor.matmul(bank(6, 0, W), con[:, C_ONE:C_ONE + P], cum[:, :], start=False, stop=True).then_inc(s_pos, 1)
                    nc.tensor.matmul(bank(6, 256, 256 + NE), con[:, C_ONE:C_ONE + P], tot[:, :], start=True, stop=True).then_inc(s_cnt, 1)

                @block.gpsimd
                def _(pool):
                    pool.wait_ge(s_tok, 16)
                    pool.wait_ge(s_ch, CH_SLOT[0])
                    for t in range(T):
                        for i in range(2):
                            nc.gpsimd.indirect_dma_start(out=idx_dram[l], out_offset=bass.IndirectOffsetOnAxis(slots[:, t, i:i + 1], 0),
                                                         in_=tok[:, t, :], in_offset=None).then_inc(s_slot, 16)
                    pool.wait_ge(s_slot, 16 * 2 * T)

        def experts(l, ring, p_in):
            C = CAP[l]
            R = C - P
            FB = D // P
            with ExitStack() as c:
                idx = sb(c, "slot_idx", [P, 2, 16], I32)
                xg = sb(c, "gathered", [P, 2, D])
                xT = sb(c, "item_xT", [P, KD, C])
                aT = sb(c, "item_aT", [P, FB, C])
                sg = sb(c, "item_silu", [P, 2, C])
                yT = sb(c, "item_yT", [P, 2, C])
                yr = sb(c, "item_y", [P, 2, D])
                s_ix, s_xg, s_xt, s_xT, s_gu, s_sg, s_a, s_y, s_yT, s_yt, s_yr, s_st, s_go = (sem(c, n) for n in (
                    "idx_in", "x_gathered", "x_transposed", "xT_ready", "gate_up", "silu_done", "hidden_ready",
                    "down_ready", "yT_ready", "y_transposed", "y_rows", "y_stored", "waited"))
                block = c.enter_context(nc.Block())
                gub = lambda b, w: bank(b % 2, w * 256, w * 256 + C)
                yb = lambda j: bank(2 + j % 2, 0, C)
                xtb = lambda r: bank(4 + r % 2)
                count = lambda eng: eng.value_load(nitem[0:1, 0:1], min_val=NE, max_val=ITEMS[l])

                @block.sync
                def _(sp):
                    n = count(sp)
                    with sp.Fori(1, n) as i:
                        e = sp.value_load(table[0:1, bass.ds(i, 1)], min_val=0, max_val=NE - 1)
                        for q in range(6):
                            if q < 4:
                                sp.wait_ge(s_gu, i * 8 + 2 * q + 2)
                            else:
                                sp.wait_ge(s_y, i * 8 + 4 * (q - 4) + 4)
                            load_piece(sp, l, ring, p_in, e, q)

                def gather(pool, j):
                    pool.dma_start(idx[:, 0, :], idx_dram[l][bass.ds(j * C, P), :]).then_inc(s_ix, 16)
                    pool.dma_start(idx[0:R, 1, :], idx_dram[l][bass.ds(j * C + P, R), :]).then_inc(s_ix, 16)
                    pool.wait_ge(s_ix, (j + 1) * 32)
                    pool.wait_ge(s_xt, j * 4 + 4)
                    pool.sem_inc(s_go, 1)
                    nc.gpsimd.indirect_dma_start(out=xg[:, 0, :], out_offset=None, in_=h_dram,
                                                 in_offset=bass.IndirectOffsetOnAxis(idx[:, 0, 0:1], 0)).then_inc(s_xg, 16)
                    nc.gpsimd.indirect_dma_start(out=xg[0:R, 1, :], out_offset=None, in_=h_dram,
                                                 in_offset=bass.IndirectOffsetOnAxis(idx[0:R, 1, 0:1], 0)).then_inc(s_xg, 16)
                    pool.wait_ge(s_xg, (j + 1) * 32)

                @block.gpsimd
                def _(pool):
                    n = count(pool)
                    pool.sem_inc(s_xt, 4)
                    gather(pool, 0)
                    with pool.Fori(0, n) as i:
                        gather(pool, i + 1)

                @block.tensor
                def _(pe):
                    n = count(pe)
                    pe.sem_inc(s_gu, 8)
                    pe.sem_inc(s_y, 8)

                    def transposes(j):
                        pe.wait_ge(s_xg, (j + 1) * 32)
                        for r in range(4):
                            if r >= 2:
                                pe.wait_ge(s_xT, j * 4 + r - 1)
                            for k in (2 * r, 2 * r + 1):
                                o = (k % 2) * 256
                                nc.tensor.transpose(xtb(r)[:, o:o + P], xg[:, 0, k * P:(k + 1) * P], ident)
                                m = nc.tensor.transpose(xtb(r)[:, o + P:o + C], xg[0:R, 1, k * P:(k + 1) * P], ident[0:R, 0:R])
                            m.then_inc(s_xt, 1)

                    transposes(0)
                    with pe.Fori(0, n) as i:
                        pe.wait_ge(s_xT, i * 4 + 4)
                        for b in range(FB):
                            if b % 2 == 0:
                                pe.wait_ge(p_in[b // 2], i * 32 + 32)
                            if b >= 2:
                                pe.wait_ge(s_a, i * 8 + b - 1)
                            for w in range(2):
                                for k in range(KD):
                                    m = nc.tensor.matmul(gub(b, w), ring[:, b // 2, k, w * 256 + (b % 2) * P:w * 256 + (b % 2 + 1) * P],
                                                         xT[:, k, :], start=k == 0, stop=k == KD - 1)
                            m.then_inc(s_gu, 1)
                        transposes(i + 1)

                        def back(j):
                            pe.wait_ge(s_yT, i * 8 + j + 1)
                            if j % 4 == 0:
                                pe.wait_ge(s_yr, i * 2 + j // 4 + 1)
                            o = (j % 4) * P
                            nc.tensor.transpose(bank(6, o, o + P), yT[:, j % 2, 0:P], ident)
                            m = nc.tensor.transpose(bank(7)[0:R, o:o + P], yT[:, j % 2, P:C], ident)
                            if j % 4 == 3:
                                m.then_inc(s_yt, 1)

                        pe.wait_ge(s_a, i * 8 + 8)
                        for j in range(KD):
                            if j % 4 == 0:
                                pe.wait_ge(p_in[4 + j // 4], i * 16 + 16)
                            for f in range(FB):
                                m = nc.tensor.matmul(yb(j), ring[:, 4 + j // 4, f, (j % 4) * P:(j % 4 + 1) * P], aT[:, f, :],
                                                     start=f == 0, stop=f == FB - 1)
                            m.then_inc(s_y, 1)
                            if j:
                                back(j - 1)
                        back(KD - 1)

                @block.scalar
                def _(act):
                    n = count(act)
                    act.sem_inc(s_st, 1)
                    with act.Fori(0, n) as i:
                        for b in range(FB):
                            act.wait_ge(s_gu, i * 8 + b + 9)
                            nc.scalar.activation(sg[:, b % 2, :], gub(b, 0), ACT.Silu).then_inc(s_sg, 1)
                        for j in range(KD):
                            act.wait_ge(s_y, i * 8 + j + 9)
                            nc.scalar.activation(yT[:, j % 2, :], yb(j), ACT.Copy).then_inc(s_yT, 1)
                        act.wait_ge(s_yr, i * 2 + 3)
                        act.dma_start(ys[bass.ds(i * C, P), :], yr[:, 0, :]).then_inc(s_st, 16)
                        act.dma_start(ys[bass.ds(i * C + P, R), :], yr[0:R, 1, :]).then_inc(s_st, 16)
                    act.wait_ge(s_st, n * 32 + 1)
                    act.sem_inc(s_go, 1)

                @block.vector
                def _(dve):
                    n = count(dve)
                    dve.sem_inc(s_yr, 1)

                    def take_x(j):
                        for r in range(4):
                            dve.wait_ge(s_xt, j * 4 + r + 5)
                            nc.vector.tensor_copy(xT[:, 2 * r:2 * r + 2, :],
                                                  xtb(r).rearrange("p (k c) -> p k c", c=256)[:, :, 0:C]).then_inc(s_xT, 1)

                    take_x(0)
                    with dve.Fori(0, n) as i:
                        for b in range(FB):
                            dve.wait_ge(s_sg, i * 8 + b + 1)
                            nc.vector.tensor_tensor(aT[:, b, :], sg[:, b % 2, :], gub(b, 1), ALU.mult).then_inc(s_a, 1)
                        take_x(i + 1)
                        for h in range(2):
                            dve.wait_ge(s_yt, i * 2 + h + 1)
                            if h == 0:
                                dve.wait_ge(s_st, i * 32 + 1)
                            nc.vector.tensor_copy(yr[0:R, 1, h * HALF:(h + 1) * HALF], bank(7)[0:R, :])
                            nc.vector.tensor_copy(yr[:, 0, h * HALF:(h + 1) * HALF], bank(6)).then_inc(s_yr, 1)

        modulation()
        x = sb(top, "x_res", [P, NT, D])
        for l in range(2):
            with ExitStack() as c:
                hT = sb(c, "hT", [P, KD, NTOK])
                wq = sb(c, "w_group", [P, 3, KD, P])
                w_in = sem(c, "w_group_in")
                normed(l, "mix", NT, "combine" if l else None, hT=hT, wq=wq, w_in=w_in)
                oT = sb(c, "oT", [P, KD * NTOK])
                wo_in = sem(c, "wo_in")
                (neighbourhood if l == 0 else differential)(hT, oT, wo_in, wq, w_in)
                rw = sb(c, "router_w", [P, KD, NE])
                normed(l, "ffn", TILES[l], "project", rw=rw, attn=(oT, hT, wo_in))
            with ExitStack() as c:
                ring = sb(c, "expert_ring", [P, 6, KD, HALF])
                p_in = [sem(c, f"piece_in{n}") for n in range(6)]
                routing(l, ring, p_in)
                experts(l, ring, p_in)
            if l == 0:
                nc.all_engine_barrier()
                nc.clear_and_free_semaphores(list(stage_sems))
                nc.all_engine_barrier()
        normed(1, "final", LT, "combine")


_INS = ["x", "c", "ctx", "c_ctx", "mod_w", "mod_b", "norm_mix", "norm_ffn", "w_qkv", "w_o", "diff_lambda", "diff_subln",
        "router_w", "router_b", "expert_w_gate", "expert_w_up", "expert_w_down", "final_norm"]


def kernel(**inputs):
    import numpy as _np
    import concourse.bacc as _bacc
    from concourse import mybir as _mybir
    from concourse.bass_utils import run_bass_kernel_spmd as _run

    nc = _bacc.Bacc("TRN2", target_bir_lowering=False, num_devices=1)
    host = {name: _np.ascontiguousarray(inputs[name]) for name in _INS}
    host["consts"], host["trig"], host["tokens"] = shape_constants()
    rpb = _np.ascontiguousarray(inputs["na_rpb"])[0]
    pad = _np.zeros((16, 15, P), _np.float32)
    pad[:, :, GRID_W - WIN_COLS:GRID_W + WIN_COLS - 1] = rpb
    host["rpb_pad"] = pad
    arrays, args = {}, {}
    for name, v in host.items():
        arrays[f"in_{name}"] = v
        args[name] = nc.dram_tensor(f"in_{name}", v.shape, _mybir.dt.from_np(v.dtype), kind="ExternalInput").ap()
    args["out"] = nc.dram_tensor("out_0", (1, SEQ, D), _mybir.dt.float32, kind="ExternalOutput").ap()
    build(nc, args)
    r = _run(nc, [arrays], core_ids=[0])
    return r.results[0]["out_0"]
```
